# Optimizing a Trainium2 kernel written in Bass

```python
import jax, jax.numpy as jnp
from jax import lax
import numpy as np

D_MODEL = 1024
BATCH = 1
SEQ = 128
DEPTH = 2
DEC_BATCH = 1
DEC_SEQ = 512
PAST_LEN = 256

GRID_W = 64
NORM_EPS = 1e-6
RW_HEADS = 8
RW_HEAD = 64
RW_WIDTH = RW_HEADS * RW_HEAD
RW_DECAY_RANK = 64
RW_A_RANK = 64
RW_GN_EPS = 64e-5
GLA_HEADS = 4
GLA_DK = 64
GLA_DV = 128
GLA_KW = GLA_HEADS * GLA_DK
GLA_VW = GLA_HEADS * GLA_DV
GLA_GATE_RANK = 16
GLA_LOGIT_NORM = 16.0
GLA_CHUNK = 64
MLA_HEADS = 8
MLA_NOPE = 64
MLA_ROPE = 32
MLA_V = 64
MLA_Q_RANK = 256
MLA_KV_RANK = 128
MLA_VW = MLA_HEADS * MLA_V
ROPE_THETA = 10000.0
ATTN_Q_BLOCK = 128
N_BRANCH = 3
IN_SIZES = (RW_WIDTH, RW_WIDTH, RW_WIDTH, RW_DECAY_RANK, RW_A_RANK, RW_WIDTH,
            GLA_KW, GLA_KW, GLA_VW, GLA_GATE_RANK, GLA_VW,
            MLA_Q_RANK, MLA_KV_RANK, MLA_ROPE, MLA_VW,
            N_BRANCH * D_MODEL)
IN_WIDTH = sum(IN_SIZES)
IN_SPLITS = tuple(int(v) for v in np.cumsum(IN_SIZES)[:-1])

kernel_name = "hybrid_rwkv7_gla_mla_diffusion_step"

F32 = jnp.float32

def rmsnorm(x, g):
    xf = x.astype(F32)
    y = xf * lax.rsqrt(jnp.mean(xf * xf, axis=-1, keepdims=True) + NORM_EPS)
    return y.astype(x.dtype) * g

def adaln_project(x, cvec, norm_g, w_mod, b_mod, w_in):
    mod = (jax.nn.silu(cvec) @ w_mod + b_mod)[:, None, :]
    shift, scale, gate = jnp.split(mod, 3, axis=-1)
    h = rmsnorm(x, norm_g) * (1 + scale) + shift
    return h @ w_in, gate

def rwkv7_scan(r, decay, k, v, kk, a, s0):
    xs = tuple(jnp.moveaxis(t.astype(F32), 1, 0) for t in (r, decay, k, v, kk, a))

    def step(s, inp):
        r_t, w_t, k_t, v_t, kk_t, a_t = inp
        sa = jnp.einsum('bhij,bhj->bhi', s, -kk_t)
        s = (s * w_t[:, :, None, :] + sa[..., None] * (kk_t * a_t)[:, :, None, :]
             + v_t[..., None] * k_t[:, :, None, :])
        return s, jnp.einsum('bhij,bhj->bhi', s, r_t)

    s_fin, out = lax.scan(step, s0.astype(F32), xs)
    return jnp.moveaxis(out, 0, 1), s_fin

def rwkv7_branch(pr, pk, pv, pwd, pad, s0, w0, w2, a0, a2, k_k, k_a, r_k, ln_g, ln_b):
    B, T, _ = pr.shape
    heads = lambda t: t.reshape(B, T, RW_HEADS, RW_HEAD)
    r, k, v = heads(pr), heads(pk), heads(pv)
    kk = (k * k_k.reshape(RW_HEADS, RW_HEAD)).astype(F32)
    kk = kk / jnp.maximum(jnp.sqrt(jnp.sum(kk * kk, -1, keepdims=True)), 1e-12)
    tw = jnp.tanh(pwd)
    outs, states = [], []
    for d in range(2):
        w_log = -jax.nn.softplus(-(w0[d] + tw @ w2[d]).astype(F32)) - 0.5
        decay = heads(jnp.exp(-jnp.exp(w_log)))
        a = heads(jax.nn.sigmoid(a0[d] + pad @ a2[d]))
        kd = k * (1 + (a - 1) * k_a.reshape(RW_HEADS, RW_HEAD))
        seqs = (r, decay, kd, v, kk, a)
        if d == 1:
            seqs = tuple(jnp.flip(t, 1) for t in seqs)
        o, s = rwkv7_scan(*seqs, s0[:, d])
        if d == 1:
            o = jnp.flip(o, 1)
        outs.append(o)
        states.append(s)
    o = outs[0] + outs[1]
    mu = jnp.mean(o, -1, keepdims=True)
    var = jnp.mean(jnp.square(o - mu), -1, keepdims=True)
    o = (o - mu) * lax.rsqrt(var + RW_GN_EPS)
    o = o * ln_g.reshape(RW_HEADS, RW_HEAD) + ln_b.reshape(RW_HEADS, RW_HEAD)
    bonus = jnp.sum(r * k * r_k, -1, keepdims=True) * v
    o = o.astype(pr.dtype) + bonus
    return o.reshape(B, T, RW_WIDTH), jnp.stack(states, 1).astype(pr.dtype)

def gla_chunk_scan(q, k, v, g, s0):
    B, T, H, _ = q.shape
    nc = T // GLA_CHUNK
    chunks = lambda t: t.astype(F32).reshape(B, nc, GLA_CHUNK, H, t.shape[-1]).transpose(1, 0, 3, 2, 4)
    lower = jnp.tril(jnp.ones((GLA_CHUNK, GLA_CHUNK), bool))[:, :, None]

    def step(s, inp):
        qc, kc, vc, gc = inp
        b = jnp.cumsum(gc, axis=2)
        b_last = b[:, :, -1:, :]
        inter = jnp.einsum('bhcd,bhde->bhce', qc * jnp.exp(b), s)
        diff = jnp.where(lower, b[:, :, :, None, :] - b[:, :, None, :, :], -jnp.inf)
        att = jnp.einsum('bhtd,bhsd,bhtsd->bhts', qc, kc, jnp.exp(diff))
        out = inter + att @ vc
        s = (s * jnp.exp(b_last).swapaxes(-1, -2)
             + jnp.einsum('bhsd,bhse->bhde', kc * jnp.exp(b_last - b), vc))
        return s, out

    s_fin, out = lax.scan(step, s0.astype(F32), (chunks(q), chunks(k), chunks(v), chunks(g)))
    out = out.transpose(1, 0, 3, 2, 4).reshape(B, T, H, v.shape[-1])
    return out, s_fin

def gla_branch(pq, pk, pv, pad, s0, a2, ab, norm_g):
    B, T, _ = pq.shape
    q = pq.reshape(B, T, GLA_HEADS, GLA_DK) * (GLA_DK ** -0.5)
    k = pk.reshape(B, T, GLA_HEADS, GLA_DK)
    v = pv.reshape(B, T, GLA_HEADS, GLA_DV)
    outs, states = [], []
    for d in range(2):
        g = jax.nn.log_sigmoid((pad @ a2[d] + ab[d]).astype(F32)) / GLA_LOGIT_NORM
        seqs = (q, k, v, g.reshape(B, T, GLA_HEADS, GLA_DK))
        if d == 1:
            seqs = tuple(jnp.flip(t, 1) for t in seqs)
        o, s = gla_chunk_scan(*seqs, s0[:, d])
        if d == 1:
            o = jnp.flip(o, 1)
        outs.append(o)
        states.append(s)
    o = rmsnorm(outs[0] + outs[1], norm_g).astype(pq.dtype)
    return o.reshape(B, T, GLA_VW), jnp.stack(states, 1).astype(pq.dtype)

def rope_tables(T):
    n_rows = T // GRID_W
    rows = jnp.repeat(jnp.arange(n_rows), GRID_W)
    cols = jnp.tile(jnp.arange(GRID_W), n_rows)
    n_freq = MLA_ROPE // 4
    inv = ROPE_THETA ** (-jnp.arange(n_freq, dtype=F32) / n_freq)
    ang = jnp.stack([rows[:, None] * inv, cols[:, None] * inv], axis=1)
    return jnp.cos(ang), jnp.sin(ang)

def apply_rope_2d(x, cos, sin):
    xs = x.reshape(x.shape[:-1] + (2, 2, MLA_ROPE // 4))
    x1, x2 = xs[..., 0, :], xs[..., 1, :]
    out = jnp.stack([x1 * cos - x2 * sin, x2 * cos + x1 * sin], axis=-2)
    return out.reshape(x.shape).astype(x.dtype)

def mla_keys(ckv, wkv_up):
    B, S, _ = ckv.shape
    kv = (ckv @ wkv_up).reshape(B, S, MLA_HEADS, MLA_NOPE + MLA_V)
    return kv[..., :MLA_NOPE], kv[..., MLA_NOPE:]

def mla_attend(q_nope, segs):
    B, T = q_nope.shape[:2]
    nb = T // ATTN_Q_BLOCK
    blk = lambda t: jnp.moveaxis(t.reshape((B, nb, ATTN_Q_BLOCK) + t.shape[2:]), 1, 0)
    scale = (MLA_NOPE + MLA_ROPE) ** -0.5
    lengths = [s[1].shape[1] for s in segs]
    cuts = [int(c) for c in np.cumsum(lengths)[:-1]]

    def one(qs):
        qn, qps = qs
        logits = [jnp.einsum('bqhd,bkhd->bhqk', qn, kn) + jnp.einsum('bqhr,bkr->bhqk', qp, kp)
                  for qp, (_, kn, kp, _) in zip(qps, segs)]
        p = jax.nn.softmax(jnp.concatenate(logits, -1).astype(F32) * scale, axis=-1).astype(q_nope.dtype)
        pieces = jnp.split(p, cuts, axis=-1)
        out = jnp.einsum('bhqk,bkhd->bqhd', pieces[0], segs[0][3])
        for pp, seg in zip(pieces[1:], segs[1:]):
            out = out + jnp.einsum('bhqk,bkhd->bqhd', pp, seg[3])
        return out

    out = lax.map(one, (blk(q_nope), tuple(blk(s[0]) for s in segs)))
    return jnp.moveaxis(out, 0, 1).reshape(B, T, MLA_VW)

def layer_forward(x, cvec, lp, ctx):
    B, T, _ = x.shape
    proj, gate = adaln_project(x, cvec, lp['norm_g'], lp['w_mod'], lp['b_mod'], lp['w_in'])
    (rw_r, rw_k, rw_v, rw_wd, rw_ad, rw_g, gl_q, gl_k, gl_v, gl_ad, gl_g,
     ml_qd, ml_kvd, ml_kpe, ml_g, merge) = jnp.split(proj, IN_SPLITS, axis=-1)
    if ctx is None:
        s_rw0 = jnp.zeros((B, 2, RW_HEADS, RW_HEAD, RW_HEAD), x.dtype)
        s_gla0 = jnp.zeros((B, 2, GLA_HEADS, GLA_DK, GLA_DV), x.dtype)
    else:
        s_rw0, s_gla0 = ctx[2], ctx[3]
    o_a, st_rw = rwkv7_branch(rw_r, rw_k, rw_v, rw_wd, rw_ad, s_rw0, lp['rw_w0'], lp['rw_w2'], lp['rw_a0'],
                              lp['rw_a2'], lp['rw_k_k'], lp['rw_k_a'], lp['rw_r_k'], lp['rw_ln_g'], lp['rw_ln_b'])
    o_b, st_gla = gla_branch(gl_q, gl_k, gl_v, gl_ad, s_gla0, lp['gla_a2'], lp['gla_ab'], lp['gla_norm_g'])
    q = (rmsnorm(ml_qd, lp['mla_qn_g']) @ lp['mla_wq_up']).reshape(B, T, MLA_HEADS, MLA_NOPE + MLA_ROPE)
    q_nope, q_pe = q[..., :MLA_NOPE], q[..., MLA_NOPE:]
    ckv = rmsnorm(ml_kvd, lp['mla_kvn_g'])
    k_nope, v = mla_keys(ckv, lp['mla_wkv_up'])
    if ctx is None:
        o_c = mla_attend(q_nope, ((q_pe, k_nope, ml_kpe, v),))
    else:
        cos, sin = rope_tables(T)
        q_rot = apply_rope_2d(q_pe, cos[:, None], sin[:, None])
        k_rot = apply_rope_2d(ml_kpe, cos, sin)
        ck_nope, cv = mla_keys(ctx[0], lp['mla_wkv_up'])
        o_c = mla_attend(q_nope, ((q_rot, k_nope, k_rot, v), (q_pe, ck_nope, ctx[1], cv)))
    y_a = (o_a * jax.nn.silu(rw_g)) @ lp['rw_out']
    y_b = (o_b * jax.nn.silu(gl_g)) @ lp['gla_out']
    y_c = (o_c * jax.nn.silu(ml_g)) @ lp['mla_out']
    g_a, g_b, g_c = jnp.split(jax.nn.sigmoid(merge), N_BRANCH, axis=-1)
    y = (g_a * y_a + g_b * y_b + g_c * y_c) @ lp['w_out']
    return x + gate * y, (ckv, ml_kpe, st_rw, st_gla)

def setup_inputs(seed: int = 0) -> dict:
    key = jax.random.key(seed)
    ks = iter(jax.random.split(key, 40))
    nrm = lambda shape, s=1.0: jax.random.normal(next(ks), shape, F32) * s
    D = D_MODEL
    H_QK = MLA_HEADS * (MLA_NOPE + MLA_ROPE)
    H_KV = MLA_HEADS * (MLA_NOPE + MLA_V)
    return {
        "x_prompt": nrm((BATCH, SEQ, D)),
        "x_sample": nrm((DEC_BATCH, DEC_SEQ, D)),
        "c": nrm((DEC_BATCH, D)),
        "cache_ckv": nrm((DEC_BATCH, DEPTH, PAST_LEN, MLA_KV_RANK)),
        "cache_kpe": nrm((DEC_BATCH, DEPTH, PAST_LEN, MLA_ROPE)),
        "state_rwkv": nrm((DEC_BATCH, DEPTH, 2, RW_HEADS, RW_HEAD, RW_HEAD)),
        "state_gla": nrm((DEC_BATCH, DEPTH, 2, GLA_HEADS, GLA_DK, GLA_DV)),
        "c_ctx": nrm((D,)),
        "norm_g": 1.0 + nrm((DEPTH, D), 0.05),
        "w_mod": nrm((DEPTH, D, 3 * D), 0.5 * D ** -0.5),
        "b_mod": nrm((DEPTH, 3 * D), 0.02),
        "w_in": nrm((DEPTH, D, IN_WIDTH), D ** -0.5),
        "rw_w0": -2.0 + nrm((DEPTH, 2, RW_WIDTH), 1.0),
        "rw_w2": nrm((DEPTH, 2, RW_DECAY_RANK, RW_WIDTH), 0.5 * RW_DECAY_RANK ** -0.5),
        "rw_a0": nrm((DEPTH, 2, RW_WIDTH), 0.5),
        "rw_a2": nrm((DEPTH, 2, RW_A_RANK, RW_WIDTH), 0.5 * RW_A_RANK ** -0.5),
        "rw_k_k": 0.85 + nrm((DEPTH, RW_WIDTH), 0.1),
        "rw_k_a": 1.0 + nrm((DEPTH, RW_WIDTH), 0.1),
        "rw_r_k": nrm((DEPTH, RW_HEADS, RW_HEAD), 0.1),
        "rw_ln_g": 1.0 + nrm((DEPTH, RW_WIDTH), 0.05),
        "rw_ln_b": nrm((DEPTH, RW_WIDTH), 0.02),
        "rw_out": nrm((DEPTH, RW_WIDTH, D), RW_WIDTH ** -0.5),
        "gla_a2": nrm((DEPTH, 2, GLA_GATE_RANK, GLA_KW), GLA_GATE_RANK ** -0.5),
        "gla_ab": nrm((DEPTH, 2, GLA_KW), 0.5),
        "gla_norm_g": 1.0 + nrm((DEPTH, GLA_DV), 0.05),
        "gla_out": nrm((DEPTH, GLA_VW, D), GLA_VW ** -0.5),
        "mla_qn_g": 1.0 + nrm((DEPTH, MLA_Q_RANK), 0.05),
        "mla_wq_up": nrm((DEPTH, MLA_Q_RANK, H_QK), MLA_Q_RANK ** -0.5),
        "mla_kvn_g": 1.0 + nrm((DEPTH, MLA_KV_RANK), 0.05),
        "mla_wkv_up": nrm((DEPTH, MLA_KV_RANK, H_KV), MLA_KV_RANK ** -0.5),
        "mla_out": nrm((DEPTH, MLA_VW, D), MLA_VW ** -0.5),
        "w_out": nrm((DEPTH, D, D), D ** -0.5),
        "final_g": 1.0 + nrm((D,), 0.05),
    }

def reference(x_prompt, x_sample, c, cache_ckv, cache_kpe, state_rwkv, state_gla, c_ctx,
              norm_g, w_mod, b_mod, w_in, rw_w0, rw_w2, rw_a0, rw_a2, rw_k_k, rw_k_a, rw_r_k,
              rw_ln_g, rw_ln_b, rw_out, gla_a2, gla_ab, gla_norm_g, gla_out,
              mla_qn_g, mla_wq_up, mla_kvn_g, mla_wkv_up, mla_out, w_out, final_g):
    hp, hs = x_prompt, x_sample
    ckv_l, kpe_l, rw_l, gla_l = [], [], [], []
    for l in range(DEPTH):
        lp = dict(norm_g=norm_g[l], w_mod=w_mod[l], b_mod=b_mod[l], w_in=w_in[l],
                  rw_w0=rw_w0[l], rw_w2=rw_w2[l], rw_a0=rw_a0[l], rw_a2=rw_a2[l], rw_k_k=rw_k_k[l],
                  rw_k_a=rw_k_a[l], rw_r_k=rw_r_k[l], rw_ln_g=rw_ln_g[l], rw_ln_b=rw_ln_b[l], rw_out=rw_out[l],
                  gla_a2=gla_a2[l], gla_ab=gla_ab[l], gla_norm_g=gla_norm_g[l], gla_out=gla_out[l],
                  mla_qn_g=mla_qn_g[l], mla_wq_up=mla_wq_up[l], mla_kvn_g=mla_kvn_g[l],
                  mla_wkv_up=mla_wkv_up[l], mla_out=mla_out[l], w_out=w_out[l])
        hp, (ckv, kpe, s_rw, s_gla) = layer_forward(hp, c_ctx[None, :], lp, None)
        ckv_l.append(ckv)
        kpe_l.append(kpe)
        rw_l.append(s_rw)
        gla_l.append(s_gla)
        ctx = (cache_ckv[:, l], cache_kpe[:, l], state_rwkv[:, l], state_gla[:, l])
        hs, _ = layer_forward(hs, c, lp, ctx)
    y_prompt = rmsnorm(hp, final_g)
    y_sample = rmsnorm(hs, final_g)
    new_ckv = jnp.stack(ckv_l, axis=1)
    new_kpe = jnp.stack(kpe_l, axis=1)
    new_rwkv = jnp.stack(rw_l, axis=1)
    new_gla = jnp.stack(gla_l, axis=1)
    return (y_prompt, y_sample, new_ckv, new_kpe, new_rwkv, new_gla)


_drawn_inputs = setup_inputs


def setup_inputs(seed=0):
    import zlib

    import numpy as np

    out = dict(_drawn_inputs(seed))
    spreads = {}
    factors = {'cache_ckv': 8.0,
     'cache_kpe': 8.0,
     'state_rwkv': 4.834,
     'state_gla': 8.0,
     'rw_ln_g': 7.068,
     'rw_ln_b': 8.0,
     'gla_norm_g': 6.661,
     'mla_qn_g': 8.0,
     'mla_wq_up': 3.172}
    for name, (base, spread) in spreads.items():
        noise = np.random.default_rng([zlib.crc32(name.encode()), seed]).standard_normal(out[name].shape)
        drawn = base * np.exp(spread * noise) if base else spread * noise
        out[name] = __import__('jax').numpy.asarray(drawn.astype(out[name].dtype))
    for name, factor in factors.items():
        out[name] = (out[name] * factor).astype(out[name].dtype)
    return out
```

```python
from contextlib import ExitStack

import numpy as np

import concourse.bass as bass
from concourse import mybir

F32 = mybir.dt.float32
U8 = mybir.dt.uint8
ACT = mybir.ActivationFunctionType
ALU = mybir.AluOpType
AX = mybir.AxisListType

P = 128
D = 1024
KT = D // P
TS, TP = 512, 128
T = TS + TP
NT = T // P
DEPTH = 2
PAST = 256
HEADS = 8
PAIRS = 4
GROUPS = ((0, 1), (2, 3), (4,))
LEVELS = (64, 32, 16, 8, 4, 2, 1)
SCALE = float(64 + 32) ** -0.5
KEYS = TS + PAST
DECAY = float(np.exp(-0.5))
RING = 5
UNIT = KT * P
NTMP = 8862 + 16 * 512

_names = (("w0", 8), ("a0", 8), ("k_k", 4), ("k_a", 4), ("r_k", 4), ("ln_g", 4), ("ln_b", 4), ("ab", 4),
          ("gla_g", 1), ("qn_g", 2), ("kvn_g", 1), ("norm_g", 8), ("b_mod", 24), ("c", 16), ("final_g", 8))
VEC, NV = {}, 0
for _n, _k in _names:
    VEC[_n] = NV
    NV += _k

_small = (("w2a2", 1024), ("gla_a2", 512), ("wq", 1536), ("wk", 512), ("wv", 512), ("ckv", PAST), ("kpe", PAST),
          ("s_rw", 8 * P), ("s_gla", 4 * P))
SM, NSM = {}, 0
for _n, _k in _small:
    SM[_n] = NSM
    NSM += _k

RW_ITEMS = [("wdad", 0)] + [(n, i) for i in range(4) for n in ("k", "r", "v", "g")]
REST_ITEMS = ([("misc", 0)] + [("gq", i) for i in range(2)] + [("gk", i) for i in range(2)]
              + [("gv", i) for i in range(4)] + [("gg", i) for i in range(4)]
              + [("qd", i) for i in range(2)] + [("kvd", 0)] + [("mg", i) for i in range(4)])
UNITS = ([("mod", i) for i in range(24)] + RW_ITEMS + REST_ITEMS
         + [u for n in range(8) for u in (("ma", n), ("oab", n), ("mb", n), ("mc", n), ("oc", n))]
         + [("wo", n) for n in range(8)])
NU = len(UNITS)
SLOT = {("g", i): i for i in range(4)}
SLOT.update({(n, i): 4 + 3 * i + j for i in range(4) for j, n in enumerate("krv")})
SLOT[("wdad", 0)] = 16
SLOT.update({it: 4 + j for j, it in enumerate(REST_ITEMS)})
GATES = ("g", "gg", "mg")

M_X, M_XT, M_OFF, M_INC, M_STR, M_LEVEL, M_ID = 0, 1, 2, 3, 4, 5, 12
NM = 13


def mask_table():
    s, t = np.meshgrid(np.arange(P), np.arange(P), indexing="ij")
    m = np.zeros((P, NM, 2, P), np.float32)
    same = (s ^ t) < 16
    for d in range(2):
        before = (s < t) if d == 0 else (s > t)
        after = (s > t) if d == 0 else (s < t)
        m[:, M_XT, d] = before & same
        m[:, M_X, d] = after & same
        m[:, M_OFF, d] = after & ~same
        m[:, M_INC, d] = before | (s == t)
        m[:, M_STR, d] = before
        for j, h in enumerate(LEVELS):
            m[:, M_LEVEL + j, d] = before & ((s ^ t) >= h) & ((s ^ t) < 2 * h)
        m[:, M_ID, d] = s == t
    return m.reshape(P, -1)


C_ID, C_ONES, C_BD, C_ROT, C_COS, C_SIN, C_BIAS = 0, 128, 256, 384, 416, 928, 1440
NC = 1448


def constant_table():
    c = np.zeros((P, NC), np.float32)
    c[:, C_ID:C_ID + P] = np.eye(P)
    c[:, C_ONES:C_ONES + P] = 1.0
    c[:, C_BD:C_BD + P] = np.kron(np.eye(2), np.ones((64, 64)))
    n_freq = 8
    inv = np.float32(10000.0) ** (-np.arange(n_freq, dtype=np.float32) / np.float32(n_freq))
    pos = [np.arange(TS) // 64, np.arange(TS) % 64]
    for r in range(32):
        axis, half, f = r // 16, r // 8 % 2, r % 8
        ang = (pos[axis].astype(np.float32) * inv[f]).astype(np.float32)
        c[64 + r, C_COS:C_COS + TS] = np.cos(ang)
        c[64 + r, C_SIN:C_SIN + TS] = np.sin(ang) * (-1.0 if half == 0 else 1.0)
        c[64 + r, C_ROT + (r ^ 8)] = 1.0
    for j, b in enumerate((1e-6, 64e-5, 0.5 * 20 * np.log(2.0), 1.0)):
        c[:, C_BIAS + j] = b
    return c


class Signal:

    def __init__(self, sem, name, values, seen):
        self.sem, self.name, self.values, self.seen, self.n = sem, name, values, seen, 0

    def mark(self, *key):
        self.n += 1
        self.values[self.name, key[0] if len(key) == 1 else key] = self.n
        return 1

    def __getitem__(self, key):
        return self.seen.get((self.name, key), 1)


def build(nc, a, seen):
    values = {}
    ctx = ExitStack()
    with ctx:
        def sb(name, shape, dt=F32):
            return ctx.enter_context(nc.sbuf_tensor(name, shape, dt))

        def sem(name):
            return ctx.enter_context(nc.semaphore(name))

        def signal(name):
            return Signal(sem(name), name, values, seen)

        psum = ctx.enter_context(nc.psum_tensor("psum", [P, 8 * 512], F32))
        hT = sb("hT", [P, KT, T])
        ring = sb("ring", [P, RING, UNIT])
        small = sb("small_sb", [P, NSM])
        vec = sb("vec_sb", [P, NV])
        con = sb("con_sb", [P, NC])
        masks = sb("masks_sb", [P, NM, 2, P], U8)
        acts = sb("acts", [P, 24, T])
        gate = sb("gate", [P, T])
        sc = sb("sc", [P, KT, 2])
        sc_t = sb("sc_t", [P, KT, 2])
        mod = sb("mod", [P, 24, 2])
        gs = sb("gs", [P, KT, 2])
        omka = sb("omka", [P, 4])
        tmp = sb("tmp", [P, NTMP])

        ident = con[:, C_ID:C_ID + P]
        ones = con[:, C_ONES:C_ONES + P]
        bd = con[:, C_BD:C_BD + P]

        def bias(j, p=slice(0, P)):
            return con[p, C_BIAS + j:C_BIAS + j + 1]

        def v(name, i=0, p=slice(0, P)):
            return vec[p, VEC[name] + i:VEC[name] + i + 1]

        def item(name, i=0):
            return acts[:, SLOT[name, i], :]

        def area(at, *shape):
            n = int(np.prod(shape))
            assert at + n <= NTMP, (at, shape)
            x = tmp[:, at:at + n]
            if len(shape) == 2:
                x = x.rearrange("p (a b) -> p a b", a=shape[0])
            elif len(shape) == 3:
                x = x.rearrange("p (a b c) -> p a b c", a=shape[0], b=shape[1])
            return x
        fac = area(0, 8, T)
        A_, R_, B_, K_ = range(4)
        w_kk, w_sw, w_ys, w_a, w_e = (area(5120 + T * j, T) for j in range(5))
        stt = area(8320, 2, 2, NT)
        trn = area(8340, 2, NT)
        st = area(8350, 2, P)
        st_t = area(8606, 2, P)
        NAMES = ["XT", "X", "Off", "AakT", "ArbT", "ArkT", "G", "H", "I", "J", "K", "TB", "TA"]

        def gbuf(g, name):
            k = NAMES.index(name)
            if g == 0:
                return area(8862 + 512 * k, 4, P)
            if k < 3:
                return area(8862 + 512 * (13 + k), 4, P)
            rest = acts[:, 17:24, :].rearrange("p a b -> p (a b)")
            if k < 11:
                o = 512 * (k - 3)
                return rest[:, o:o + 512].rearrange("p (a b) -> p a b", a=4)
            o = 512 * (k - 11)
            return gate2[:, o:o + 512].rearrange("p (a b) -> p a b", a=4)
        gate2 = sb("gate2", [P, 1024])
        sraw = sb("sraw", [P, 2, 2, NT])

        w_rs = area(0, T)
        g_qi = [area(0, T), area(640, T)]
        g_ki = area(1280, T)
        g_kit = area(1920, NT, P)
        g_vt = area(2560, 10, P)
        g_st = [area(3840, NT, P), area(4480, NT, P)]
        g_att = [area(5120, 10, P), area(6400, 10, P)]
        g_kl = [area(7680, T), area(8320, T)]
        g_ql = [area(8960, T), area(9600, T)]
        g_b, g_z = area(10240, T), area(10880, T)
        g_e = [area(11520, T), area(12160, T)]
        g_d, g_x, g_ax = area(12800, T), area(13440, T), area(14080, T)
        g_eq, g_ek = g_e
        g_osq, g_o = area(14720, T), area(15360, T)
        g_new = area(16000, 4, P)
        g_dec = sb("g_dec", [P, NT])
        m_sq = [area(T * j, T) for j in range(3)]
        m_k = [area(1920, KEYS + TP), area(2816, KEYS + TP)]
        m_qp = [area(3712, T), area(4352, T)]
        m_qr = [area(4992, TS), area(5504, TS)]
        m_v = area(6016, 7, 512)
        m_p = [area(9600, KEYS), area(10368, KEYS)]
        m_pt = [area(11136, KEYS), area(11904, KEYS)]
        m_t = area(12672, T)
        m_r = [area(13312, T), area(13952, T)]
        m_nm, m_sum, m_rec = (sb(n, [P, HEADS * NT]) for n in ("m_nm", "m_sum", "m_rec"))
        yT = area(0, KT, T)
        xres = [area(5120, T), area(5760, T)]
        f_s = [area(14400 + T * j, T) for j in range(3)]
        f_t = [area(12672, T), area(16320, T)]

        s_con = sem("constants_loaded")
        s_small = sem("layer_weights_loaded")
        s_x = sem("x_loaded")
        s_unit = [sem(f"unit{j}_loaded") for j in range(RING)]
        s_out = sem("outputs_written")
        s_sto = sem("states_written")
        s_gst = sem("gla_states_written")
        s_keep = sem("x_kept")
        s_xres = [sem(f"x_reloaded{j}") for j in range(2)]
        filled = signal("psum_filled")
        act_e = signal("act_emptied")
        dve_e = signal("dve_emptied")
        used = signal("unit_used")
        act_step = signal("act_step")
        dve_step = signal("dve_step")
        act_J = signal("act_J")
        act_ex = signal("act_ex")
        act_gexp = signal("act_gexp")
        act_gln = signal("act_gln")
        act_grs = signal("act_grs")
        act_kvrs = signal("act_kvrs")
        act_le = signal("act_le")
        act_ors = signal("act_ors")
        act_qrs = signal("act_qrs")
        act_rn = signal("act_rn")
        act_sc = signal("act_sc")
        act_sig = signal("act_sig")
        act_tanh = signal("act_tanh")
        act_xrs = signal("act_xrs")
        dve_FT = signal("dve_FT")
        dve_MT1 = signal("dve_MT1")
        dve_ckv = signal("dve_ckv")
        dve_fac = signal("dve_fac")
        dve_gax = signal("dve_gax")
        dve_gla_out = signal("dve_gla_out")
        dve_gosq = signal("dve_gosq")
        dve_gstates = signal("dve_gstates")
        dve_gz = signal("dve_gz")
        dve_h = signal("dve_h")
        dve_ki = signal("dve_ki")
        dve_kksq = signal("dve_kksq")
        dve_kpe = signal("dve_kpe")
        dve_kq = signal("dve_kq")
        dve_kvsq = signal("dve_kvsq")
        dve_lvl = signal("dve_lvl")
        dve_new_state = signal("dve_new_state")
        dve_nm = signal("dve_nm")
        dve_osq = signal("dve_osq")
        dve_pn = signal("dve_pn")
        dve_qn = signal("dve_qn")
        dve_qr = signal("dve_qr")
        dve_qsq = signal("dve_qsq")
        dve_rkr = signal("dve_rkr")
        dve_rwkv_done = signal("dve_rwkv_done")
        dve_sc = signal("dve_sc")
        dve_state = signal("dve_state")
        dve_state_done = signal("dve_state_done")
        dve_xsq = signal("dve_xsq")
        dve_y = signal("dve_y")
        dve_ysum = signal("dve_ysum")
        dve_yz = signal("dve_yz")
        dve_zeroed = signal("dve_zeroed")
        pool_g1 = signal("pool_g1")
        pool_gate = signal("pool_gate")
        pool_gla_stored = signal("pool_gla_stored")
        emptied = {"act": act_e, "dve": dve_e}

        book = {"at": 0, "list": []}

        def ticket(pe, key, banks, by):
            at = book["at"]
            if at % 8 + banks > 8:
                at += 8 - at % 8
            for old, o_at, o_banks, o_by in reversed(book["list"]):
                if o_at + 8 < at + banks and o_at + o_banks + 8 > at:
                    pe.wait_ge(emptied[o_by].sem, emptied[o_by][old])
                elif o_at + o_banks + 8 <= at:
                    break
            book["list"].append((key, at, banks, by))
            book["at"] = at + banks
            values["at", key] = at % 8
            return at % 8 * 512

        def place(key):
            return seen.get(("at", key), 0) * 512

        block = ctx.enter_context(nc.Block())

        @block.sync
        def _(sp):
            sp.dma_start(con[:, :], a["con"]).then_inc(s_con, 16)
            sp.dma_start(area(0, NM * 2 * P), a["masks"]).then_inc(s_con, 16)
            for l in range(DEPTH):
                for u in range(NU):
                    n = l * NU + u
                    if n >= RING:
                        ol, ou = divmod(n - RING, NU)
                        name, i = UNITS[ou]
                        if name == "mod" and i < 23:
                            sp.wait_ge(used.sem, used[(ol, i)])
                        elif name == "mod":
                            sp.wait_ge(filled.sem, filled[("mod", ol)])
                        elif (name, i) in SLOT:
                            sp.wait_ge(filled.sem, filled[(ol, name, i)])
                        else:
                            sp.wait_ge(filled.sem, filled[({"oab": "yb", "oc": "yc"}.get(name, name), ol, i)])
                    sp.dma_start(ring[:, n % RING, :], a["units"][l, u]).then_inc(s_unit[n % RING], 16)

        @block.gpsimd
        def _(pool):
            for l in range(DEPTH):
                if l:
                    pool.wait_ge(filled.sem, filled[("mlaO", l - 1, 7, 4)])
                    pool.wait_ge(dve_e.sem, dve_e[("wo", l - 1, 7)])
                pool.dma_start(small[:, :], a["small"][l]).then_inc(s_small, 16)
                pool.dma_start(vec[:, :], a["vec"][l]).then_inc(s_small, 16)
                if l == 0:
                    pool.dma_start(hT[:, :, :], a["xT"]).then_inc(s_x, 16)
                    pool.memset(gate[:, :], 1.0)
                    pool.memset(gate2[:, :], 0.0).then_inc(pool_g1.sem, pool_g1.mark(0))
                    pool.wait_ge(pool_g1.sem, pool_g1[0])
                    pool.wait_ge(s_con, 32)
                    pool.tensor_copy(masks[:, :, :, :].rearrange("p a b c -> p (a b c)"), area(0, NM * 2 * P))
                    pool.memset(gate[:, ::P], 0.0).then_inc(pool_gate.sem, pool_gate.mark(0))
                for p in range(PAIRS):
                    pool.wait_ge(dve_new_state.sem, dve_new_state[l, p])
                    pool.dma_start(a["new_rw"][l, p], st_t.rearrange("p a b -> p (a b)")).then_inc(s_sto, 16)
                for p in range(2):
                    for d in range(2):
                        pool.wait_ge(dve_e.sem, dve_e[("gs", l, p, d)])
                pool.dma_start(a["new_gla"][l], g_new.rearrange("p a b -> p (a b)")).then_inc(s_gst, 16)
                pool.wait_ge(s_gst, 16 * (l + 1))
                pool.memset(gate2[:, 0:1], 0.0).then_inc(pool_gla_stored.sem, pool_gla_stored.mark(l))
                pool.wait_ge(act_e.sem, act_e[(l, "misc", 0)])
                pool.dma_start(a["new_kpe"][l], item("misc")[64:96, TS:T]).then_inc(s_out, 16)
                pool.wait_ge(dve_ckv.sem, dve_ckv[l])
                pool.dma_start(a["new_ckv"][l], item("kvd")[:, TS:T]).then_inc(s_out, 16)
                pool.wait_ge(dve_e.sem, dve_e[("mlaO", l, 7, 4)])
                x_old = a["xT"] if l == 0 else a["x_keep"]
                for n in range(KT):
                    if n >= 2:
                        pool.wait_ge(dve_e.sem, dve_e[("wo", l, n - 2)])
                    pool.dma_start(xres[n % 2], x_old[:, n, :]).then_inc(s_xres[n % 2], 16)
                    if l == 0 and n >= 2:
                        pool.dma_start(a["x_keep"][:, n - 2, :], hT[:, n - 2, :]).then_inc(s_keep, 16)
                if l == 0:
                    for n in (KT - 2, KT - 1):
                        pool.wait_ge(dve_e.sem, dve_e[("wo", l, n)])
                        pool.dma_start(a["x_keep"][:, n, :], hT[:, n, :]).then_inc(s_keep, 16)
            for n in range(KT):
                pool.wait_ge(dve_y.sem, dve_y[n])
                pool.dma_start(a["yT"][:, n, :], acts[:, n, :]).then_inc(s_out, 16)
            pool.wait_ge(s_out, 16 * (2 * DEPTH + KT))
            pool.wait_ge(s_sto, 16 * DEPTH * PAIRS)
            pool.wait_ge(s_keep, 16 * KT)

        @block.tensor
        def _(pe):
            def mm(out, lhsT, rhs, start, stop):
                return nc.tensor.matmul(out, lhsT, rhs, start=start, stop=stop, skip_group_check=True)

            def tr(out, in_, p=P):
                return nc.tensor.transpose(out, in_, ident[0:p, 0:p])

            def wide(at, lhsT, rhs, start=True, stop=True, m=slice(0, P)):
                mm(psum[m, at:at + TS], lhsT, rhs[:, 0:TS], start, stop)
                return mm(psum[m, at + TS:at + T], lhsT, rhs[:, TS:T], start, stop)

            count = [0]

            def unit():
                n = count[0]
                pe.wait_ge(s_unit[n % RING], 16 * (n // RING + 1))
                return ring[:, n % RING, :].rearrange("p (k n) -> p k n", k=KT)

            def unit_done():
                count[0] += 1

            def project(l, it):
                w = unit()
                key = (l, *it)
                at = ticket(pe, key, 2, "dve" if it[0] in GATES else "act")
                for k in range(KT):
                    mm(psum[:, at:at + TS], w[:, k, :], hT[:, k, 0:TS], k == 0, k == KT - 1)
                for k in range(KT):
                    last = mm(psum[:, at + TS:at + T], w[:, k, :], hT[:, k, TS:T], k == 0, k == KT - 1)
                last.then_inc(filled.sem, filled.mark(key))
                unit_done()

            def sums(key, lhsT, rhs_list, by="act"):
                at = ticket(pe, key, 2, by)
                for j, r in enumerate(rhs_list):
                    last = wide(at, lhsT, r, j == 0, j == len(rhs_list) - 1)
                last.then_inc(filled.sem, filled.mark(key))

            pe.wait_ge(s_con, 32)

            for l in range(DEPTH):
                pe.wait_ge(s_small, 32 * (l + 1))
                pe.wait_ge(dve_sc.sem, dve_sc[0])
                at = ticket(pe, ("mod", l), 1, "dve")
                for u in range(24):
                    w = unit()
                    for k in range(KT):
                        last = mm(psum[:, at + 2 * u:at + 2 * u + 2], w[:, k, :], sc[:, k, :], k == 0, k == KT - 1)
                    if u == 23:
                        last.then_inc(filled.sem, filled.mark(("mod", l)))
                    else:
                        last.then_inc(used.sem, used.mark((l, u)))
                    unit_done()
                at = ticket(pe, ("xss", l), 2, "act")
                for k in range(KT):
                    pe.wait_ge(dve_xsq.sem, dve_xsq[l, k])
                    last = wide(at, ones, acts[:, k, :], k == 0, k == KT - 1)
                last.then_inc(filled.sem, filled.mark(("xss", l)))
                for k in range(KT):
                    pe.wait_ge(dve_h.sem, dve_h[l, k])
                for it in RW_ITEMS:
                    project(l, it)

                pe.wait_ge(act_e.sem, act_e[(l, "wdad", 0)])
                pe.wait_ge(act_tanh.sem, act_tanh[l])
                for p in range(PAIRS):
                    pe.wait_ge(dve_kksq.sem, dve_kksq[l, p])
                    sums(("kkss", l, p), bd, [w_ys], by="dve")
                    for d in range(2):
                        for n, rows in (("zw", slice(0, 64)), ("za", slice(64, 128))):
                            at = ticket(pe, (n, l, p, d), 2, "act")
                            w = small[rows, SM["w2a2"] + 512 * d + P * p:SM["w2a2"] + 512 * d + P * p + P]
                            wide(at, w, item("wdad")[rows, :]).then_inc(filled.sem, filled.mark((n, l, p, d)))
                    for d in range(2):
                        pe.wait_ge(dve_fac.sem, dve_fac[l, p, d])
                    for steps in GROUPS:
                        def tile(d, s):
                            return s if s == 4 or d == 0 else 3 - s

                        def cols(d, s):
                            return slice(P * tile(d, s), P * tile(d, s) + P)

                        def F(d, kind, s):
                            return fac[:, 4 * d + kind, cols(d, s)]

                        def units():
                            return [(u, u // 2, slice(64 * (u % 2), 64 * (u % 2) + 64)) for u in range(4)]

                        def each(s, key, by, f):
                            at = ticket(pe, (key, l, p, s), 1, by)
                            for u in range(4):
                                lhsT, rhs = f(u)
                                last = mm(psum[:, at + P * u:at + P * u + P], lhsT, rhs, True, True)
                            last.then_inc(filled.sem, filled.mark((key, l, p, s)))

                        def got(s, *keys):
                            for key, by in keys:
                                pe.wait_ge(emptied[by].sem, emptied[by][(key, l, p, s)])

                        for s in steps:
                            at = ticket(pe, ("TB", l, p, s), 1, "act")
                            for d in range(2):
                                tr(psum[:, at + 256 * d:at + 256 * d + P], F(d, B_, s))
                                last = tr(psum[:, at + 256 * d + P:at + 256 * d + 256], F(d, K_, s))
                            last.then_inc(filled.sem, filled.mark(("TB", l, p, s)))
                            at = ticket(pe, ("TA", l, p, s), 1, "act")
                            for d in range(2):
                                tr(psum[:, at + 256 * d:at + 256 * d + P], F(d, A_, s))
                                last = tr(psum[:, at + 256 * d + P:at + 256 * d + 256], item("v", p)[:, cols(d, s)])
                            last.then_inc(filled.sem, filled.mark(("TA", l, p, s)))
                        for s in steps:
                            for key, kind, rhs in (("Ab", B_, (A_, R_)), ("Ak", K_, (A_, R_)), ("Aab", A_, (B_, B_))):
                                at = ticket(pe, (key, l, p, s), 2, "dve")
                                n = rhs[1] - rhs[0] + 1
                                for d in range(2):
                                    moving = fac[:, 4 * d + rhs[0]:4 * d + rhs[1] + 1, cols(d, s)]
                                    for h in range(2):
                                        hs = slice(64 * h, 64 * h + 64)
                                        o = at + 512 * h + 256 * d
                                        last = mm(psum[:, o:o + P * n], F(d, kind, s)[hs, :], moving[hs], True, True)
                                last.then_inc(filled.sem, filled.mark((key, l, p, s)))

                        def B(s, name):
                            g = gbuf(s % 2, name)
                            return lambda u: g[:, u, :]
                        for s in steps:
                            got(s, ("Ab", "dve"), ("Aab", "dve"))
                            each(s, "X2", "act", lambda u: (B(s, "XT")(u), B(s, "X")(u)))
                            each(s, "X2T", "act", lambda u: (B(s, "X")(u), B(s, "XT")(u)))
                        for s in steps:
                            got(s, ("X2", "act"), ("X2T", "act"))
                            pe.wait_ge(dve_FT.sem, dve_FT[l, p, s])
                            each(s, "X4", "act", lambda u: (B(s, "I")(u), B(s, "H")(u)))
                            each(s, "X4T", "act", lambda u: (B(s, "H")(u), B(s, "I")(u)))
                            each(s, "GT", "dve", lambda u: (B(s, "H")(u), B(s, "G")(u)))
                        for s in steps:
                            got(s, ("X4", "act"), ("X4T", "act"), ("GT", "dve"))
                            each(s, "X8", "act", lambda u: (B(s, "XT")(u), B(s, "X")(u)))
                            each(s, "HT", "dve", lambda u: (B(s, "X")(u), B(s, "G")(u)))
                        for s in steps:
                            got(s, ("X8", "act"), ("HT", "dve"))
                            each(s, "T16T", "dve", lambda u: (B(s, "H")(u), B(s, "G")(u)))
                        for s in steps:
                            got(s, ("T16T", "dve"), ("Ak", "dve"), ("TA", "act"))
                            each(s, "NT", "act", lambda u: (B(s, "Off")(u), B(s, "G")(u)))
                            each(s, "N", "act", lambda u: (B(s, "G")(u), B(s, "Off")(u)))
                            at = ticket(pe, ("AV", l, p, s), 1, "act")
                            for u in range(4):
                                d, h = u // 2, u % 2
                                last = mm(psum[:, at + 64 * u:at + 64 * u + 64], B(s, "AakT")(u),
                                          gbuf(s % 2, "TA")[:, 2 * d + 1, 64 * h:64 * h + 64], True, True)
                            last.then_inc(filled.sem, filled.mark(("AV", l, p, s)))
                        for s in steps:
                            got(s, ("NT", "act"), ("N", "act"), ("AV", "act"))
                            each(s, "N2", "act", lambda u: (B(s, "I")(u), B(s, "H")(u)))
                            each(s, "N2T", "act", lambda u: (B(s, "H")(u), B(s, "I")(u)))
                            pe.wait_ge(act_J.sem, act_J[l, p, s])
                            each(s, "Y1", "dve", lambda u: (B(s, "G")(u), B(s, "J")(u)))
                        for s in steps:
                            got(s, ("N2", "act"), ("N2T", "act"))
                            pe.wait_ge(dve_MT1.sem, dve_MT1[l, p, s])
                            each(s, "N4", "act", lambda u: (B(s, "AakT")(u), B(s, "Off")(u)))
                            each(s, "MT2", "dve", lambda u: (B(s, "Off")(u), B(s, "I")(u)))
                        for s in steps:
                            got(s, ("N4", "act"), ("MT2", "dve"))
                            each(s, "MT3", "dve", lambda u: (B(s, "H")(u), B(s, "I")(u)))
                        for s in steps:
                            got(s, ("MT3", "dve"), ("Y1", "dve"))
                            each(s, "Y", "act", lambda u: (B(s, "I")(u), B(s, "K")(u)))
                        for s in steps:
                            got(s, ("Y", "act"))
                            at = ticket(pe, ("TaT", l, p, s), 1, "act")
                            for d in range(2):
                                last = tr(psum[:, at + P * d:at + P * d + P], gbuf(s % 2, "J")[:, d, :])
                            last.then_inc(filled.sem, filled.mark(("TaT", l, p, s)))
                        for s in steps:
                            got(s, ("TaT", "act"), ("TB", "act"))
                            pe.wait_ge(dve_state.sem, dve_state[l, p, s])
                            K, TA, TB = gbuf(s % 2, "K"), gbuf(s % 2, "TA"), gbuf(s % 2, "TB")
                            at = ticket(pe, ("U", l, p, s), 1, "dve")
                            for d in range(2):
                                last = mm(psum[:, at + P * d:at + P * d + P], K[:, d, :], st[:, d, :], True, True)
                            last.then_inc(filled.sem, filled.mark(("U", l, p, s)))
                            got(s, ("U", "dve"))
                            at = ticket(pe, ("S", l, p, s), 1, "dve") if s != 3 else None
                            for d in range(2) if s != 3 else ():
                                mm(psum[:, at + P * d:at + P * d + P], TB[:, 2 * d, :], K[:, 2 + d, :], True, False)
                                last = mm(psum[:, at + P * d:at + P * d + P], TB[:, 2 * d + 1, :],
                                          TA[:, 2 * d + 1, :], False, True)
                            if s != 3:
                                last.then_inc(filled.sem, filled.mark(("S", l, p, s)))
                            at = ticket(pe, ("O", l, p, s), 1, "dve")
                            for d in range(2):
                                o = psum[:, at + P * d:at + P * d + P]
                                mm(o, st[:, d, :], F(d, R_, s), True, False)
                                for h in range(2):
                                    u, hs = 2 * d + h, slice(64 * h, 64 * h + 64)
                                    mm(psum[hs, at + P * d:at + P * d + P], K[:, 2 + d, hs], B(s, "ArbT")(u),
                                       False, False)
                                    last = mm(psum[hs, at + P * d:at + P * d + P], TA[:, 2 * d + 1, hs],
                                              B(s, "ArkT")(u), False, True)
                            last.then_inc(filled.sem, filled.mark(("O", l, p, s)))
                    pe.wait_ge(dve_e.sem, dve_e[("O", l, p, 4)])
                    sums(("omean", l, p), bd, [item("k", p)], by="dve")
                    pe.wait_ge(dve_osq.sem, dve_osq[l, p])
                    sums(("ovar", l, p), bd, [w_ys], by="act")
                    pe.wait_ge(dve_rkr.sem, dve_rkr[l, p])
                    sums(("bonus", l, p), bd, [item("r", p)], by="dve")

                for it in REST_ITEMS:
                    pe.wait_ge(dve_rwkv_done.sem, dve_rwkv_done[l])
                    project(l, it)

                pe.wait_ge(act_e.sem, act_e[(l, "gv", 3)])
                for p in range(2):
                    for h in range(2):
                        at = ticket(pe, ("gvt", l, p, h), 2, "act")
                        for i in range(NT):
                            last = tr(psum[:, at + P * i:at + P * i + P], item("gv", 2 * p + h)[:, P * i:P * i + P])
                        last.then_inc(filled.sem, filled.mark(("gvt", l, p, h)))
                    for d in range(2):
                        at = ticket(pe, ("gx", l, p, d), 2, "dve")
                        w = small[0:16, SM["gla_a2"] + 256 * d + P * p:SM["gla_a2"] + 256 * d + P * p + P]
                        wide(at, w, item("misc")[0:16, :]).then_inc(filled.sem, filled.mark(("gx", l, p, d)))
                        pe.wait_ge(dve_ki.sem, dve_ki[l, p, d])
                        at = ticket(pe, ("kit", l, p, d), 2, "act")
                        for i in range(NT):
                            last = tr(psum[:, at + P * i:at + P * i + P], g_ki[:, P * i:P * i + P])
                        last.then_inc(filled.sem, filled.mark(("kit", l, p, d)))
                        pe.wait_ge(act_e.sem, act_e[("kit", l, p, d)])
                        pe.wait_ge(act_e.sem, act_e[("gvt", l, p, 1)])
                        at = ticket(pe, ("gs", l, p, d), 2, "dve")
                        for i in range(NT):
                            for h in range(2):
                                hs = slice(64 * h, 64 * h + 64)
                                last = mm(psum[hs, at + P * i:at + P * i + P], g_kit[:, i, hs], g_vt[:, 5 * h + i, :],
                                          True, True)
                        last.then_inc(filled.sem, filled.mark(("gs", l, p, d)))
                        for j in range(8):
                            if j < 7:
                                pe.wait_ge(dve_kq.sem, dve_kq[l, p, d, j])
                                kl, ql = g_kl[j % 2], g_ql[j % 2]
                            else:
                                kl, ql = item("gk", p), item("gq", p)
                            ats = [ticket(pe, ("att", l, p, d, j, h), 2, "dve") for h in range(2)]
                            for i in range(NT):
                                for h in range(2):
                                    hs = slice(64 * h, 64 * h + 64)
                                    last = mm(psum[:, ats[h] + P * i:ats[h] + P * i + P], kl[hs, P * i:P * i + P],
                                              ql[hs, P * i:P * i + P], True, True)
                                    if i == NT - 1:
                                        last.then_inc(filled.sem, filled.mark(("att", l, p, d, j, h)))
                    for h in range(2):
                        hs = slice(64 * h, 64 * h + 64)
                        at = ticket(pe, ("go", l, p, h), 2, "dve")
                        pe.wait_ge(dve_e.sem, dve_e[("att", l, p, 1, 7, 1)])
                        pe.wait_ge(dve_gstates.sem, dve_gstates[l, p, 1])
                        for i in range(NT):
                            o = psum[:, at + P * i:at + P * i + P]
                            for d in range(2):
                                mm(o, g_st[d][hs, i, :], g_qi[d][hs, P * i:P * i + P], d == 0, False)
                                last = mm(o, g_vt[:, 5 * h + i, :], g_att[d][:, 5 * h + i, :], False, d == 1)
                        last.then_inc(filled.sem, filled.mark(("go", l, p, h)))
                        pe.wait_ge(dve_gosq.sem, dve_gosq[l, p, h])
                        sums(("goss", l, p, h), ones, [g_osq], by="act")

                for j in range(2):
                    pe.wait_ge(dve_qsq.sem, dve_qsq[l, j])
                sums(("qss", l), ones, [m_sq[0], m_sq[1]])
                pe.wait_ge(dve_kvsq.sem, dve_kvsq[l])
                sums(("kvss", l), ones, [m_sq[2]])
                pe.wait_ge(act_e.sem, act_e[(l, "misc", 0)])
                at = ticket(pe, ("krot", l), 1, "dve")
                mm(psum[64:96, at:at + TS], con[64:96, C_ROT:C_ROT + 32], item("misc")[64:96, 0:TS],
                             True, True).then_inc(filled.sem, filled.mark(("krot", l)))
                pe.wait_ge(dve_ckv.sem, dve_ckv[l])
                for i in range(7):
                    src = (item("kvd")[:, P * i:P * i + P] if i < 4 else
                           small[:, SM["ckv"] + P * (i - 4):SM["ckv"] + P * (i - 3)] if i < 6 else
                           item("kvd")[:, TS:T])
                    at = ticket(pe, ("mv", l, i), 1, "act")
                    mm(psum[:, at:at + 512], src, small[:, SM["wv"]:SM["wv"] + 512], True, True).then_inc(filled.sem, filled.mark(("mv", l, i)))

                def head_qk(h):
                    at = ticket(pe, ("mk", l, h), 2, "act")
                    w = small[:, SM["wk"] + 64 * h:SM["wk"] + 64 * h + 64]
                    mm(psum[0:64, at:at + TS], w, item("kvd")[:, 0:TS], True, True)
                    mm(psum[0:64, at + TS:at + KEYS], w, small[:, SM["ckv"]:SM["ckv"] + PAST], True, True)
                    mm(psum[0:64, at + KEYS:at + KEYS + TP], w, item("kvd")[:, TS:T], True, True).then_inc(filled.sem, filled.mark(("mk", l, h)))
                    at = ticket(pe, ("mq", l, h), 2, "act")
                    for k in range(2):
                        w = small[:, SM["wq"] + 768 * k + 96 * h:SM["wq"] + 768 * k + 96 * h + 96]
                        last = wide(at, w, item("qd", k), k == 0, k == 1, m=slice(0, 96))
                    last.then_inc(filled.sem, filled.mark(("mq", l, h)))

                def head_rot(h):
                    pe.wait_ge(act_e.sem, act_e[("mq", l, h)])
                    at = ticket(pe, ("qrot", l, h), 1, "dve")
                    mm(psum[64:96, at:at + TS], con[64:96, C_ROT:C_ROT + 32], m_qp[h % 2][64:96, 0:TS],
                                 True, True).then_inc(filled.sem, filled.mark(("qrot", l, h)))

                def logits(h, i):
                    pe.wait_ge(act_e.sem, act_e[("mk", l, h)])
                    pe.wait_ge(dve_qr.sem, dve_qr[l, h])
                    q = slice(P * i, P * i + P)
                    k = m_k[h % 2]
                    if i < 4:
                        at = ticket(pe, ("lg", l, h, i), 2, "act")
                        mm(psum[:, at:at + TS], m_qr[h % 2][0:96, q], k[0:96, 0:TS], True, True)
                        last = mm(psum[:, at + TS:at + KEYS], m_qp[h % 2][0:96, q], k[0:96, TS:KEYS], True, True)
                    else:
                        at = ticket(pe, ("lg", l, h, i), 2, "act")
                        last = mm(psum[:, at:at + TP], m_qp[h % 2][0:96, q], k[0:96, KEYS:KEYS + TP], True, True)
                    last.then_inc(filled.sem, filled.mark(("lg", l, h, i)))

                def turn(h, i):
                    pe.wait_ge(dve_pn.sem, dve_pn[l, h, i])
                    at = ticket(pe, ("pt", l, h, i), 2, "act")
                    for j in range(6 if i < 4 else 1):
                        last = tr(psum[:, at + P * j:at + P * j + P], m_p[(5 * h + i) % 2][:, P * j:P * j + P])
                    last.then_inc(filled.sem, filled.mark(("pt", l, h, i)))

                def weigh(h, i):
                    pe.wait_ge(act_e.sem, act_e[("pt", l, h, i)])
                    hs = slice(64 * (h % 2), 64 * (h % 2) + 64)
                    at = ticket(pe, ("mlaO", l, h, i), 1, "dve")
                    ks = range(6) if i < 4 else [6]
                    for j, kt in enumerate(ks):
                        last = mm(psum[hs, at:at + P], m_v[:, kt, 64 * h:64 * h + 64],
                                  m_pt[(5 * h + i) % 2][:, P * j:P * j + P], j == 0, j == len(ks) - 1)
                    last.then_inc(filled.sem, filled.mark(("mlaO", l, h, i)))

                for key in [("mv", l, 6)]:
                    pe.wait_ge(act_e.sem, act_e[key])
                for k in range(2):
                    pe.wait_ge(dve_qn.sem, dve_qn[l, k])
                pe.wait_ge(dve_kpe.sem, dve_kpe[l])
                steps = [(h, i) for h in range(HEADS) for i in range(NT)]
                head_qk(0)
                head_rot(0)
                for n in range(len(steps) + 2):
                    if n < len(steps):
                        if steps[n][1] == 2 and steps[n][0] + 1 < HEADS:
                            if steps[n][0] >= 1:
                                pass
                            head_qk(steps[n][0] + 1)
                        if steps[n][1] == 3 and steps[n][0] + 1 < HEADS:
                            head_rot(steps[n][0] + 1)
                        logits(*steps[n])
                    if 1 <= n <= len(steps):
                        turn(*steps[n - 1])
                    if n >= 2:
                        weigh(*steps[n - 2])

                for n in range(KT):
                    def merge(key):
                        w = unit()
                        at = ticket(pe, (key, l, n), 2, "act")
                        for k in range(KT):
                            last = wide(at, w[:, k, :], hT[:, k, :], k == 0, k == KT - 1)
                        last.then_inc(filled.sem, filled.mark((key, l, n)))
                        unit_done()

                    def branch(key, w, o):
                        at = ticket(pe, (key, l, n), 2, "dve")
                        for k in range(4):
                            last = wide(at, w[:, k, :], acts[:, o + k, :], k == 0, k == 3)
                        last.then_inc(filled.sem, filled.mark((key, l, n)))
                    merge("ma")
                    w = unit()
                    branch("ya", w[:, 0:4, :], SLOT["g", 0])
                    branch("yb", w[:, 4:8, :], SLOT["gg", 0])
                    unit_done()
                    merge("mb")
                    merge("mc")
                    pe.wait_ge(dve_e.sem, dve_e[("mlaO", l, 7, 4)])
                    w = unit()
                    branch("yc", w[:, 0:4, :], SLOT["mg", 0])
                    unit_done()
                for n in range(KT):
                    if n == 0:
                        for m in range(KT):
                            pe.wait_ge(dve_ysum.sem, dve_ysum[l, m])
                    w = unit()
                    at = ticket(pe, ("wo", l, n), 2, "dve")
                    for k in range(KT):
                        last = wide(at, w[:, k, :], yT[:, k, :], k == 0, k == KT - 1)
                    last.then_inc(filled.sem, filled.mark(("wo", l, n)))
                    unit_done()
            at = ticket(pe, ("xss", DEPTH), 2, "act")
            for k in range(KT):
                pe.wait_ge(dve_xsq.sem, dve_xsq[DEPTH, k])
                last = wide(at, ones, acts[:, k, :], k == 0, k == KT - 1)
            last.then_inc(filled.sem, filled.mark(("xss", DEPTH)))

        @block.scalar
        def _(act):

            def rstd(key, out, scale, eps):
                act.wait_ge(filled.sem, filled[key])
                at = place(key)
                ins = nc.scalar.activation(out, psum[:, at:at + T], ACT.Ln, bias=con[:, C_BIAS + eps:C_BIAS + eps + 1],
                                           scale=scale)
                ins.then_inc(act_e.sem, act_e.mark(key))
                act.wait_ge(act_e.sem, act_e[key])
                return nc.scalar.activation(out, out, ACT.Exp, scale=-0.5)

            def copy(key, out, src, scale=None):
                if scale is None:
                    nc.scalar.activation(out, src, ACT.Copy).then_inc(act_e.sem, act_e.mark(key))
                else:
                    nc.scalar.activation(out, src, ACT.Copy, scale=scale).then_inc(act_e.sem, act_e.mark(key))

            act.wait_ge(s_small, 32)
            act.wait_ge(s_con, 32)
            nc.scalar.activation(sc_t[:, :, :].rearrange("p a b -> p (a b)"), vec[:, VEC["c"]:VEC["c"] + 16],
                                             ACT.Sigmoid).then_inc(act_sc.sem, act_sc.mark(0))

            def project(l, it):
                act.wait_ge(filled.sem, filled[(l, *it)])
                at = place((l, *it))
                src = psum[:, at:at + T]
                if it[0] in GATES:
                    nc.scalar.activation(item(*it), src, ACT.Sigmoid).then_inc(act_sig.sem, act_sig.mark(l, it))
                elif it[0] == "wdad":
                    nc.scalar.activation(item(*it)[0:64, :], psum[0:64, at:at + T], ACT.Tanh).then_inc(act_tanh.sem, act_tanh.mark(l))
                    copy((l, *it), item(*it)[64:128, :], psum[64:128, at:at + T])
                else:
                    copy((l, *it), item(*it), src, 0.125 if it[0] == "gq" else None)

            for l in range(DEPTH):
                rstd(("xss", l), w_rs, 1.0 / D, 0).then_inc(act_xrs.sem, act_xrs.mark(l))
                act.wait_ge(s_small, 32 * (l + 1))
                act.wait_ge(dve_zeroed.sem, dve_zeroed[l])
                for it in RW_ITEMS:
                    project(l, it)
                for p in range(PAIRS):
                    act.wait_ge(dve_e.sem, dve_e[("kkss", l, p)])
                    nc.scalar.activation(w_ys, w_ys, ACT.Ln, scale=2.0 ** 20).then_inc(act_step.sem, act_step.mark())
                    act.wait_ge(act_step.sem, act_step.n)
                    nc.scalar.activation(w_ys, w_ys, ACT.Exp, scale=-0.5,
                                                     bias=con[:, C_BIAS + 2:C_BIAS + 3]).then_inc(act_rn.sem, act_rn.mark(l, p))
                    for d in range(2):
                        if d == 1:
                            act.wait_ge(dve_fac.sem, dve_fac[l, p, 0])
                        act.wait_ge(filled.sem, filled[("zw", l, p, d)])
                        at = place(("zw", l, p, d))
                        nc.scalar.activation(w_sw, psum[:, at:at + T], ACT.Sigmoid, bias=v("w0", 4 * d + p)).then_inc(act_e.sem, act_e.mark(("zw", l, p, d)))
                        act.wait_ge(filled.sem, filled[("za", l, p, d)])
                        at = place(("za", l, p, d))
                        nc.scalar.activation(w_a, psum[:, at:at + T], ACT.Sigmoid, bias=v("a0", 4 * d + p)).then_inc(act_e.sem, act_e.mark(("za", l, p, d)))
                        act.wait_ge(dve_yz.sem, dve_yz[l, p, d])
                        src, sign = ((w_ys, w_sw, w_ys), (-DECAY, -DECAY, DECAY)) if d == 0 else \
                                    ((w_sw, w_ys, w_sw), (DECAY, DECAY, -DECAY))
                        nc.scalar.activation(fac[:, 4 * d + R_, :], src[0], ACT.Exp, scale=sign[0])
                        nc.scalar.activation(fac[:, 4 * d + A_, :], src[1], ACT.Exp, scale=sign[1])
                        nc.scalar.activation(w_e, src[2], ACT.Exp, scale=sign[2])
                        nc.scalar.activation(stt[:, d, :, :], sraw[:, d, :, :], ACT.Exp, scale=-DECAY).then_inc(act_ex.sem, act_ex.mark(l, p, d))
                    for steps in GROUPS:
                        def bank(key, s, n=512):
                            act.wait_ge(filled.sem, filled[(key, l, p, s)])
                            at = place((key, l, p, s))
                            return psum[:, at:at + n]

                        def flat(s, name):
                            return gbuf(s % 2, name).rearrange("p a b -> p (a b)")

                        def out(s, key, name):
                            copy((key, l, p, s), flat(s, name), bank(key, s))
                        for s in steps:
                            out(s, "TB", "TB")
                            out(s, "TA", "TA")
                        for s in steps:
                            out(s, "X2", "H")
                            out(s, "X2T", "I")
                        for s in steps:
                            out(s, "X4", "X")
                            out(s, "X4T", "XT")
                        for s in steps:
                            out(s, "X8", "H")
                        for s in steps:
                            out(s, "NT", "I")
                            out(s, "N", "H")
                            J, TA = gbuf(s % 2, "J"), gbuf(s % 2, "TA")
                            copy(("AV", l, p, s), J[:, :, 64:128],
                                 bank("AV", s, 256).rearrange("p (u i) -> p u i", u=4))
                            act.wait_ge(act_e.sem, act_e[("TA", l, p, s)])
                            for d in range(2):
                                ins = nc.scalar.activation(J[:, 2 * d:2 * d + 2, 0:64],
                                                           TA[:, 2 * d, :].rearrange("p (h i) -> p h i", h=2), ACT.Copy)
                            ins.then_inc(act_J.sem, act_J.mark(l, p, s))
                        for s in steps:
                            out(s, "N2", "Off")
                            out(s, "N2T", "AakT")
                        for s in steps:
                            out(s, "N4", "H")
                        for s in steps:
                            J = gbuf(s % 2, "J").rearrange("p (w d) x -> p w (d x)", w=2)
                            src = bank("Y", s).rearrange("p (u w x) -> p w u x", u=4, w=2)
                            nc.scalar.activation(J[:, 0, :].rearrange("p (u x) -> p u x", u=4), src[:, 0, :, :], ACT.Copy)
                            copy(("Y", l, p, s), J[:, 1, :].rearrange("p (u x) -> p u x", u=4), src[:, 1, :, :])
                        for s in steps:
                            copy(("TaT", l, p, s), flat(s, "K")[:, 0:256], bank("TaT", s, 256))
                    rstd(("ovar", l, p), w_sw, 1.0 / 64, 1).then_inc(act_ors.sem, act_ors.mark(l, p))

                for it in REST_ITEMS:
                    project(l, it)

                for p in range(2):
                    for h in range(2):
                        act.wait_ge(filled.sem, filled[("gvt", l, p, h)])
                        at = place(("gvt", l, p, h))
                        copy(("gvt", l, p, h), g_vt[:, 5 * h:5 * h + 5, :].rearrange("p a b -> p (a b)"),
                             psum[:, at:at + T])
                    for d in range(2):
                        act.wait_ge(dve_gax.sem, dve_gax[l, p, d])
                        nc.scalar.activation(g_ax, g_ax, ACT.Exp, scale=-1.0).then_inc(act_step.sem, act_step.mark())
                        act.wait_ge(act_step.sem, act_step.n)
                        nc.scalar.activation(g_ax, g_ax, ACT.Ln, bias=con[:, C_BIAS + 3:C_BIAS + 4]).then_inc(act_gln.sem, act_gln.mark(l, p, d))
                        act.wait_ge(dve_gz.sem, dve_gz[l, p, d])
                        z = g_b if d == 0 else g_z
                        nc.scalar.activation(g_eq, z if d == 0 else g_d, ACT.Exp, scale=1.0 / 16)
                        nc.scalar.activation(g_ek, g_d if d == 0 else z, ACT.Exp, scale=1.0 / 16)
                        nc.scalar.activation(g_dec[:, :], g_b[:, P - 1::P], ACT.Exp, scale=1.0 / 16).then_inc(act_gexp.sem, act_gexp.mark(l, p, d))
                        act.wait_ge(filled.sem, filled[("kit", l, p, d)])
                        at = place(("kit", l, p, d))
                        copy(("kit", l, p, d), g_kit[:, :, :].rearrange("p a b -> p (a b)"), psum[:, at:at + T])
                        for j in range(7):
                            act.wait_ge(dve_lvl.sem, dve_lvl[l, p, d, j])
                            nc.scalar.activation(g_e[j % 2], g_e[j % 2], ACT.Exp, scale=1.0 / 16).then_inc(act_le.sem, act_le.mark(l, p, d, j))
                    for h in range(2):
                        if h:
                            act.wait_ge(dve_gla_out.sem, dve_gla_out[l, 2 * p])
                        rstd(("goss", l, p, h), g_ax, 1.0 / P, 0).then_inc(act_grs.sem, act_grs.mark(l, p, h))

                act.wait_ge(dve_gla_out.sem, dve_gla_out[l, 3])
                rstd(("qss", l), m_r[0], 1.0 / 256, 0).then_inc(act_qrs.sem, act_qrs.mark(l))
                rstd(("kvss", l), m_r[1], 1.0 / 128, 0).then_inc(act_kvrs.sem, act_kvrs.mark(l))
                for i in range(7):
                    act.wait_ge(filled.sem, filled[("mv", l, i)])
                    at = place(("mv", l, i))
                    copy(("mv", l, i), m_v[:, i, :], psum[:, at:at + 512])

                def head_qk(h):
                    act.wait_ge(filled.sem, filled[("mk", l, h)])
                    at = place(("mk", l, h))
                    copy(("mk", l, h), m_k[h % 2][0:64, :], psum[0:64, at:at + KEYS + TP])
                    act.wait_ge(filled.sem, filled[("mq", l, h)])
                    at = place(("mq", l, h))
                    nc.scalar.activation(m_qr[h % 2][0:64, :], psum[0:64, at:at + TS], ACT.Copy, scale=SCALE)
                    copy(("mq", l, h), m_qp[h % 2][0:96, :], psum[0:96, at:at + T], SCALE)

                steps = [(h, i) for h in range(HEADS) for i in range(NT)]
                head_qk(0)
                for n in range(len(steps) + 1):
                    if n < len(steps):
                        h, i = steps[n]
                        if i == 2 and h + 1 < HEADS:
                            head_qk(h + 1)
                        w = KEYS if i < 4 else TP
                        act.wait_ge(filled.sem, filled[("lg", l, h, i)])
                        at = place(("lg", l, h, i))
                        act.wait_ge(dve_nm.sem, dve_nm[l, h, i])
                        nc.scalar.activation(m_p[n % 2][:, 0:w], psum[:, at:at + w], ACT.Exp,
                                                      bias=m_nm[:, n:n + 1], accum_out=m_sum[:, n:n + 1]).then_inc(act_e.sem, act_e.mark(("lg", l, h, i)))
                    if n >= 1:
                        h, i = steps[n - 1]
                        w = KEYS if i < 4 else TP
                        act.wait_ge(filled.sem, filled[("pt", l, h, i)])
                        at = place(("pt", l, h, i))
                        copy(("pt", l, h, i), m_pt[(n - 1) % 2][:, 0:w], psum[:, at:at + w])
                for n in range(KT):
                    for j, (key, y) in enumerate((("ma", "ya"), ("mb", "yb"), ("mc", "yc"))):
                        if n:
                            act.wait_ge(dve_e.sem, dve_e[(y, l, n - 1)])
                        act.wait_ge(filled.sem, filled[(key, l, n)])
                        at = place((key, l, n))
                        nc.scalar.activation(f_s[j], psum[:, at:at + T], ACT.Sigmoid).then_inc(act_e.sem, act_e.mark((key, l, n)))
            rstd(("xss", DEPTH), w_rs, 1.0 / D, 0).then_inc(act_xrs.sem, act_xrs.mark(DEPTH))

        @block.vector
        def _(dve):
            V = nc.vector


            def ttn(out, a, b, op):
                return V.tensor_tensor(out, a, b, op)

            def mul(out, a, b):
                return V.tensor_tensor(out, a, b, ALU.mult)

            def ts(out, a, s1, s2=None, op0=ALU.mult, op1=None):
                if s2 is None:
                    return V.tensor_scalar(out, a, s1, None, op0)
                return V.tensor_scalar(out, a, s1, s2, op0, op1)

            def stt3(out, a, s, b, op0, op1):
                return V.scalar_tensor_tensor(out=out, in0=a, scalar=s, in1=b, op0=op0, op1=op1)

            def norm_input(l):
                for k in range(KT):
                    mul(acts[:, k, :], hT[:, k, :], hT[:, k, :]).then_inc(dve_xsq.sem, dve_xsq.mark(l, k))

            dve.wait_ge(s_small, 32)
            dve.wait_ge(act_sc.sem, act_sc[0])
            mul(sc[:, :, :].rearrange("p a b -> p (a b)"), sc_t[:, :, :].rearrange("p a b -> p (a b)"),
                            vec[:, VEC["c"]:VEC["c"] + 16]).then_inc(dve_sc.sem, dve_sc.mark(0))
            dve.wait_ge(pool_gate.sem, pool_gate[0])
            for l in range(DEPTH):
                dve.wait_ge(s_small, 32 * (l + 1))
                ts(omka[:, :], vec[:, VEC["k_a"]:VEC["k_a"] + 4], -1.0, 1.0, ALU.mult, ALU.add).then_inc(dve_step.sem, dve_step.mark())
                dve.wait_ge(dve_step.sem, dve_step.n)
                if l == 0:
                    dve.wait_ge(s_x, 16)
                norm_input(l)
                dve.wait_ge(filled.sem, filled[("mod", l)])
                at = place(("mod", l))
                ins = ttn(mod[:, :, :], psum[:, at:at + 48].rearrange("p (a b) -> p a b", a=24),
                          vec[:, VEC["b_mod"]:VEC["b_mod"] + 24].unsqueeze(2).broadcast_to([P, 24, 2]), ALU.add)
                ins.then_inc(dve_e.sem, dve_e.mark(("mod", l)))
                dve.wait_ge(dve_e.sem, dve_e[("mod", l)])
                stt3(gs[:, :, :], mod[:, 8:16, :], 1.0,
                           vec[:, VEC["norm_g"]:VEC["norm_g"] + 8].unsqueeze(2).broadcast_to([P, 8, 2]),
                           ALU.add, ALU.mult).then_inc(dve_step.sem, dve_step.mark())
                dve.wait_ge(dve_step.sem, dve_step.n)
                dve.wait_ge(act_xrs.sem, act_xrs[l])
                if l:
                    dve.wait_ge(s_keep, 16 * KT)
                for k in range(KT):
                    ins = mul(hT[:, k, :], hT[:, k, :], w_rs)
                ins.then_inc(dve_step.sem, dve_step.mark())
                dve.wait_ge(dve_step.sem, dve_step.n)
                for k in range(KT):
                    ts(hT[:, k, 0:TS], hT[:, k, 0:TS], gs[:, k, 0:1], mod[:, k, 0:1], ALU.mult, ALU.add)
                    ts(hT[:, k, TS:T], hT[:, k, TS:T], gs[:, k, 1:2], mod[:, k, 1:2],
                                   ALU.mult, ALU.add).then_inc(dve_h.sem, dve_h.mark(l, k))
                for g in range(2):
                    for name in ("XT", "X", "Off", "AakT", "ArbT", "ArkT"):
                        ins = V.memset(gbuf(g, name), 0.0)
                ins.then_inc(dve_zeroed.sem, dve_zeroed.mark(l))
                dve.wait_ge(dve_zeroed.sem, dve_zeroed[l])

                def gates(items):
                    for it in items:
                        if it[0] in GATES:
                            dve.wait_ge(filled.sem, filled[(l, *it)])
                            at = place((l, *it))
                            dve.wait_ge(act_sig.sem, act_sig[l, it])
                            mul(item(*it), item(*it), psum[:, at:at + T]).then_inc(dve_e.sem, dve_e.mark((l, *it)))
                gates(RW_ITEMS)

                for p in range(PAIRS):
                    k_, r_, v_ = item("k", p), item("r", p), item("v", p)
                    dve.wait_ge(act_e.sem, act_e[(l, "v", p)])
                    ts(w_kk, k_, v("k_k", p)).then_inc(dve_step.sem, dve_step.mark())
                    dve.wait_ge(dve_step.sem, dve_step.n)
                    mul(w_ys, w_kk, w_kk).then_inc(dve_kksq.sem, dve_kksq.mark(l, p))
                    dve.wait_ge(filled.sem, filled[("kkss", l, p)])
                    at = place(("kkss", l, p))
                    ts(w_ys, psum[:, at:at + T], 1e-24, op0=ALU.max).then_inc(dve_e.sem, dve_e.mark(("kkss", l, p)))
                    dve.wait_ge(act_rn.sem, act_rn[l, p])
                    mul(w_kk, w_kk, w_ys).then_inc(dve_step.sem, dve_step.mark())
                    dve.wait_ge(dve_step.sem, dve_step.n)
                    for d in range(2):
                        dve.wait_ge(act_e.sem, act_e[("zw", l, p, d)])
                        if d == 0 and p:
                            dve.wait_ge(dve_state_done.sem, dve_state_done[l, p - 1])
                        V.tensor_tensor_scan(w_ys, gate[:, :], w_sw, 0.0, ALU.mult, ALU.add).then_inc(dve_step.sem, dve_step.mark())
                        dve.wait_ge(dve_step.sem, dve_step.n)
                        ys3 = w_ys.rearrange("p (n t) -> p n t", n=NT)
                        ins = V.tensor_copy(sraw[:, d, 0, :], w_ys[:, 63::P])
                        ins.then_inc(dve_step.sem, dve_step.mark())
                        dve.wait_ge(dve_step.sem, dve_step.n)
                        ttn(sraw[:, d, 1, :], w_ys[:, P - 1::P], sraw[:, d, 0, :], ALU.subtract).then_inc(dve_step.sem, dve_step.mark())
                        dve.wait_ge(dve_step.sem, dve_step.n)
                        ttn(ys3, ys3, sraw[:, d, 0, :].unsqueeze(2).broadcast_to([P, NT, P]), ALU.subtract).then_inc(dve_step.sem, dve_step.mark())
                        dve.wait_ge(dve_step.sem, dve_step.n)
                        ttn(w_sw, w_ys, w_sw, ALU.subtract).then_inc(dve_yz.sem, dve_yz.mark(l, p, d))
                        dve.wait_ge(act_e.sem, act_e[("za", l, p, d)])
                        mul(fac[:, 4 * d + B_, :], w_kk, w_a)
                        ts(fac[:, 4 * d + K_, :], w_a, v("k_a", p), omka[:, p:p + 1], ALU.mult, ALU.add).then_inc(dve_step.sem, dve_step.mark())
                        dve.wait_ge(dve_step.sem, dve_step.n)
                        mul(fac[:, 4 * d + K_, :], fac[:, 4 * d + K_, :], k_).then_inc(dve_step.sem, dve_step.mark())
                        dve.wait_ge(dve_step.sem, dve_step.n)
                        dve.wait_ge(act_ex.sem, act_ex[l, p, d])
                        mul(fac[:, 4 * d + R_, :], fac[:, 4 * d + R_, :], r_)
                        stt3(fac[:, 4 * d + A_, :], fac[:, 4 * d + A_, :], -1.0, w_kk, ALU.mult, ALU.mult)
                        mul(fac[:, 4 * d + B_, :], fac[:, 4 * d + B_, :], w_e)
                        mul(fac[:, 4 * d + K_, :], fac[:, 4 * d + K_, :], w_e).then_inc(dve_fac.sem, dve_fac.mark(l, p, d))
                    mul(trn[:, 0, 0:3], stt[:, 0, 1, 0:3], stt[:, 0, 0, 1:4])
                    ins = mul(trn[:, 1, 1:4], stt[:, 1, 0, 1:4], stt[:, 1, 1, 0:3])
                    for d in range(2):
                        s0 = small[:, SM["s_rw"] + P * (4 * d + p):SM["s_rw"] + P * (4 * d + p) + P]
                        i0 = 0 if d == 0 else 3
                        ins = ts(st[:, d, :], s0, stt[:, d, d, i0:i0 + 1])
                    ins.then_inc(dve_state.sem, dve_state.mark(l, p, 0))
                    dve.wait_ge(dve_state.sem, dve_state[l, p, 0])
                    dve.wait_ge(dve_fac.sem, dve_fac[l, p, 1])
                    ts(r_, r_, v("r_k", p)).then_inc(dve_step.sem, dve_step.mark())
                    dve.wait_ge(dve_step.sem, dve_step.n)
                    mul(r_, r_, k_).then_inc(dve_rkr.sem, dve_rkr.mark(l, p))
                    dve.wait_ge(dve_rkr.sem, dve_rkr[l, p])
                    V.memset(k_, 0.0).then_inc(dve_step.sem, dve_step.mark())
                    dve.wait_ge(dve_step.sem, dve_step.n)

                    for steps in GROUPS:
                        def tile(d, s):
                            return s if s == 4 or d == 0 else 3 - s

                        def bank(key, s, n=512):
                            dve.wait_ge(filled.sem, filled[(key, l, p, s)])
                            at = place((key, l, p, s))
                            return psum[:, at:at + n]

                        def masked(s, key, w, name, m, last=True):
                            src = bank(key, s, 1024).rearrange("p (h d w x) -> p w d h x", h=2, d=2, w=2)[:, w]
                            ins = V.copy_predicated(gbuf(s % 2, name).rearrange("p (d h) x -> p d h x", d=2),
                                                    masks[:, m, :, :].unsqueeze(2).broadcast_to([P, 2, 2, P]), src)
                            if last:
                                ins.then_inc(dve_e.sem, dve_e.mark((key, l, p, s)))

                        def add(s, key, name):
                            B = gbuf(s % 2, name).rearrange("p a b -> p (a b)")
                            ttn(B, bank(key, s), B, ALU.add).then_inc(dve_e.sem, dve_e.mark((key, l, p, s)))
                        for s in steps:
                            masked(s, "Ab", 0, "XT", M_XT, last=False)
                            masked(s, "Ab", 1, "ArbT", M_INC)
                            masked(s, "Ak", 0, "AakT", M_STR, last=False)
                            masked(s, "Ak", 1, "ArkT", M_INC)
                            masked(s, "Aab", 0, "X", M_X, last=False)
                            masked(s, "Aab", 0, "Off", M_OFF)
                            dve.wait_ge(dve_e.sem, dve_e[("Ab", l, p, s)])
                            ttn(gbuf(s % 2, "G"), gbuf(s % 2, "XT"),
                                            ident.unsqueeze(1).broadcast_to([P, 4, P]), ALU.add).then_inc(dve_FT.sem, dve_FT.mark(l, p, s))
                        for s in steps:
                            dve.wait_ge(dve_FT.sem, dve_FT[l, p, s])
                            add(s, "GT", "G")
                        for s in steps:
                            dve.wait_ge(dve_e.sem, dve_e[("GT", l, p, s)])
                            add(s, "HT", "G")
                        for s in steps:
                            dve.wait_ge(dve_e.sem, dve_e[("HT", l, p, s)])
                            add(s, "T16T", "G")
                        for s in steps:
                            V.tensor_copy(gbuf(s % 2, "K").rearrange("p a b -> p (a b)"), bank("Y1", s)).then_inc(dve_e.sem, dve_e.mark(("Y1", l, p, s)))
                            dve.wait_ge(act_e.sem, act_e[("NT", l, p, s)])
                            ttn(gbuf(s % 2, "I"), gbuf(s % 2, "I"),
                                            ident.unsqueeze(1).broadcast_to([P, 4, P]), ALU.add).then_inc(dve_MT1.sem, dve_MT1.mark(l, p, s))
                        for s in steps:
                            dve.wait_ge(dve_MT1.sem, dve_MT1[l, p, s])
                            add(s, "MT2", "I")
                        for s in steps:
                            dve.wait_ge(dve_e.sem, dve_e[("MT2", l, p, s)])
                            add(s, "MT3", "I")
                        for s in steps:
                            J, K = gbuf(s % 2, "J"), gbuf(s % 2, "K")
                            src = bank("U", s, 256).rearrange("p (d x) -> p d x", d=2)
                            dve.wait_ge(act_e.sem, act_e[("Y", l, p, s)])
                            ttn(K[:, 2:4, :], src, J[:, 2:4, :], ALU.add).then_inc(dve_e.sem, dve_e.mark(("U", l, p, s)))
                            if s != 3:
                                src = bank("S", s, 256)
                                if s == 0 and l * 4 + p:
                                    dve.wait_ge(s_sto, 16 * (l * 4 + p))
                                for d in range(2):
                                    i = tile(d, s)
                                    g = (trn[:, d, i:i + 1] if s < 3 else stt[:, d, 1 - d, 4:5])
                                    ins = stt3(st_t[:, d, :], src[:, P * d:P * d + P], g, bd, ALU.mult, ALU.mult)
                                ins.then_inc(dve_e.sem, dve_e.mark(("S", l, p, s)))
                                if s == 4:
                                    V.memset(trn[:, :, :], 0.0).then_inc(dve_new_state.sem, dve_new_state.mark(l, p))
                            src = bank("O", s, 256)
                            for d in range(2):
                                o = k_[:, P * tile(d, s):P * tile(d, s) + P]
                                ins = ttn(o, o, src[:, P * d:P * d + P], ALU.add)
                                if s == 4 and d == 0:
                                    ins.then_inc(dve_step.sem, dve_step.mark())
                                    dve.wait_ge(dve_step.sem, dve_step.n)
                            ins.then_inc(dve_e.sem, dve_e.mark(("O", l, p, s)))
                            if s < 3:
                                dve.wait_ge(dve_e.sem, dve_e[("S", l, p, s)])
                                for d in range(2):
                                    i = tile(d, s)
                                    ins = stt3(st[:, d, :], st[:, d, :], trn[:, d, i:i + 1], st_t[:, d, :],
                                               ALU.mult, ALU.add)
                                ins.then_inc(dve_state.sem, dve_state.mark(l, p, s + 1))
                                dve.wait_ge(dve_state.sem, dve_state[l, p, s + 1])
                            elif s == 3:
                                V.memset(st[:, :, :], 0.0).then_inc(dve_state.sem, dve_state.mark(l, p, 4))
                    dve.wait_ge(dve_e.sem, dve_e[("O", l, p, 4)])
                    dve.wait_ge(dve_e.sem, dve_e[("O", l, p, 4)])
                    dve.wait_ge(filled.sem, filled[("omean", l, p)])
                    at = place(("omean", l, p))
                    stt3(w_kk, psum[:, at:at + T], -1.0 / 64, k_, ALU.mult, ALU.add).then_inc(dve_e.sem, dve_e.mark(("omean", l, p)))
                    dve.wait_ge(dve_e.sem, dve_e[("omean", l, p)])
                    mul(w_ys, w_kk, w_kk).then_inc(dve_osq.sem, dve_osq.mark(l, p))
                    dve.wait_ge(filled.sem, filled[("bonus", l, p)])
                    at = place(("bonus", l, p))
                    mul(w_a, psum[:, at:at + T], v_).then_inc(dve_e.sem, dve_e.mark(("bonus", l, p)))
                    dve.wait_ge(act_ors.sem, act_ors[l, p])
                    mul(w_kk, w_kk, w_sw).then_inc(dve_step.sem, dve_step.mark())
                    dve.wait_ge(dve_step.sem, dve_step.n)
                    ts(w_kk, w_kk, v("ln_g", p), v("ln_b", p), ALU.mult, ALU.add).then_inc(dve_step.sem, dve_step.mark())
                    dve.wait_ge(dve_step.sem, dve_step.n)
                    dve.wait_ge(dve_e.sem, dve_e[("bonus", l, p)])
                    ttn(w_kk, w_kk, w_a, ALU.add).then_inc(dve_step.sem, dve_step.mark())
                    dve.wait_ge(dve_step.sem, dve_step.n)
                    mul(item("g", p), item("g", p), w_kk).then_inc(dve_state_done.sem, dve_state_done.mark(l, p))
                    dve.wait_ge(dve_state_done.sem, dve_state_done[l, p])
                dve.wait_ge(s_sto, 16 * (l * 4 + 4))
                for d in range(2):
                    ins = V.memset(g_att[d], 0.0)
                ins.then_inc(dve_rwkv_done.sem, dve_rwkv_done.mark(l))
                dve.wait_ge(dve_rwkv_done.sem, dve_rwkv_done[l])
                gates(REST_ITEMS)

                for p in range(2):
                    q_, k_ = item("gq", p), item("gk", p)
                    for d in range(2):
                        dve.wait_ge(filled.sem, filled[("gx", l, p, d)])
                        at = place(("gx", l, p, d))
                        ts(g_x, psum[:, at:at + T], v("ab", 2 * d + p), op0=ALU.add).then_inc(dve_e.sem, dve_e.mark(("gx", l, p, d)))
                        dve.wait_ge(dve_e.sem, dve_e[("gx", l, p, d)])
                        stt3(g_ax, g_x, -1.0, g_x, ALU.mult, ALU.max).then_inc(dve_gax.sem, dve_gax.mark(l, p, d))
                        dve.wait_ge(act_gln.sem, act_gln[l, p, d])
                        stt3(g_z, g_x, 0.0, g_ax, ALU.min, ALU.subtract).then_inc(dve_step.sem, dve_step.mark())
                        dve.wait_ge(dve_step.sem, dve_step.n)
                        V.tensor_tensor_scan(g_b, gate[:, :], g_z, 0.0, ALU.mult, ALU.add).then_inc(dve_step.sem, dve_step.mark())
                        dve.wait_ge(dve_step.sem, dve_step.n)
                        z = g_b
                        if d == 1:
                            ttn(g_z, g_b, g_z, ALU.subtract).then_inc(dve_step.sem, dve_step.mark())
                            dve.wait_ge(dve_step.sem, dve_step.n)
                            z = g_z
                        z3 = z.rearrange("p (n t) -> p n t", n=NT)
                        b3 = g_b.rearrange("p (n t) -> p n t", n=NT)
                        ttn(g_d.rearrange("p (n t) -> p n t", n=NT),
                                        b3[:, :, P - 1:P].broadcast_to([P, NT, P]), z3, ALU.subtract).then_inc(dve_gz.sem, dve_gz.mark(l, p, d))
                        dve.wait_ge(act_gexp.sem, act_gexp[l, p, d])
                        dve.wait_ge(act_e.sem, act_e[(l, "gk", p)])
                        mul(g_qi[d], g_eq, q_)
                        mul(g_ki, g_ek, k_).then_inc(dve_ki.sem, dve_ki.mark(l, p, d))
                        dve.wait_ge(filled.sem, filled[("gs", l, p, d)])
                        at = place(("gs", l, p, d))
                        o = SM["s_gla"] + P * (2 * d + p)
                        order = (0, 1, 2, 3) if d == 0 else (3, 2, 1, 0)
                        V.memset(g_st[d][:, 4, :], 0.0)
                        V.tensor_copy(g_st[d][:, order[0], :], small[:, o:o + P]).then_inc(dve_step.sem, dve_step.mark())
                        dve.wait_ge(dve_step.sem, dve_step.n)
                        for i, j in zip(order, order[1:]):
                            stt3(g_st[d][:, j, :], g_st[d][:, i, :], g_dec[:, i:i + 1],
                                       psum[:, at + P * i:at + P * i + P], ALU.mult, ALU.add).then_inc(dve_step.sem, dve_step.mark())
                            dve.wait_ge(dve_step.sem, dve_step.n)
                        V.tensor_copy(g_new[:, 2 * p + d, :], psum[:, at + 4 * P:at + 5 * P]).then_inc(dve_e.sem, dve_e.mark(("gs", l, p, d)))
                        V.memset(g_x[:, 0:1], 0.0).then_inc(dve_gstates.sem, dve_gstates.mark(l, p, d))

                        def level(j):
                            h = LEVELS[j]
                            zz = z.rearrange("p (n c) -> p n c", c=2 * h)
                            ee = g_e[j % 2].rearrange("p (n c) -> p n c", c=2 * h)
                            ref = g_b.rearrange("p (n c) -> p n c", c=2 * h)[:, :, h - 1:h]
                            ref = ref.broadcast_to([P, T // (2 * h), h])
                            ttn(ee[:, :, 0:h], ref, zz[:, :, 0:h], ALU.subtract)
                            ttn(ee[:, :, h:2 * h], zz[:, :, h:2 * h], ref, ALU.subtract).then_inc(dve_lvl.sem, dve_lvl.mark(l, p, d, j))

                        def attention(j):
                            m = M_LEVEL + j if j < 7 else M_ID
                            mask = masks[:, m, d, :].unsqueeze(1).broadcast_to([P, NT, P])
                            for h in range(2):
                                dve.wait_ge(filled.sem, filled[("att", l, p, d, j, h)])
                                at = place(("att", l, p, d, j, h))
                                if j:
                                    dve.wait_ge(dve_e.sem, dve_e[("att", l, p, d, j - 1, h)])
                                ins = V.copy_predicated(g_att[d][:, 5 * h:5 * h + 5, :], mask,
                                                        psum[:, at:at + T].rearrange("p (n t) -> p n t", n=NT))
                                ins.then_inc(dve_e.sem, dve_e.mark(("att", l, p, d, j, h)))
                        level(0)
                        level(1)
                        for j in range(8):
                            if j < 7:
                                dve.wait_ge(act_le.sem, act_le[l, p, d, j])
                                mul(g_kl[j % 2], g_e[j % 2], k_)
                                mul(g_ql[j % 2], g_e[j % 2], q_).then_inc(dve_kq.sem, dve_kq.mark(l, p, d, j))
                                dve.wait_ge(dve_kq.sem, dve_kq[l, p, d, j])
                            if j + 2 < 7:
                                level(j + 2)
                            if j:
                                attention(j - 1)
                        attention(7)
                    for h in range(2):
                        dve.wait_ge(filled.sem, filled[("go", l, p, h)])
                        at = place(("go", l, p, h))
                        V.tensor_copy(g_o, psum[:, at:at + T]).then_inc(dve_e.sem, dve_e.mark(("go", l, p, h)))
                        dve.wait_ge(dve_e.sem, dve_e[("go", l, p, h)])
                        mul(g_osq, g_o, g_o).then_inc(dve_gosq.sem, dve_gosq.mark(l, p, h))
                        dve.wait_ge(act_grs.sem, act_grs[l, p, h])
                        mul(g_o, g_o, g_ax).then_inc(dve_step.sem, dve_step.mark())
                        dve.wait_ge(dve_step.sem, dve_step.n)
                        g_ = item("gg", 2 * p + h)
                        stt3(g_, g_o, v("gla_g"), g_, ALU.mult, ALU.mult).then_inc(dve_gla_out.sem, dve_gla_out.mark(l, 2 * p + h))
                        dve.wait_ge(dve_gla_out.sem, dve_gla_out[l, 2 * p + h])
                dve.wait_ge(pool_gla_stored.sem, pool_gla_stored[l])

                for k in range(2):
                    mul(m_sq[k], item("qd", k), item("qd", k)).then_inc(dve_qsq.sem, dve_qsq.mark(l, k))
                dve.wait_ge(act_e.sem, act_e[(l, "kvd", 0)])
                mul(m_sq[2], item("kvd"), item("kvd")).then_inc(dve_kvsq.sem, dve_kvsq.mark(l))
                dve.wait_ge(act_qrs.sem, act_qrs[l])
                for k in range(2):
                    stt3(item("qd", k), item("qd", k), v("qn_g", k), m_r[0], ALU.mult, ALU.mult).then_inc(dve_qn.sem, dve_qn.mark(l, k))
                dve.wait_ge(act_kvrs.sem, act_kvrs[l])
                stt3(item("kvd"), item("kvd"), v("kvn_g"), m_r[1], ALU.mult, ALU.mult).then_inc(dve_ckv.sem, dve_ckv.mark(l))
                rr = slice(64, 96)
                dve.wait_ge(filled.sem, filled[("krot", l)])
                at = place(("krot", l))
                mul(m_t[rr, 0:TS], psum[rr, at:at + TS], con[rr, C_SIN:C_SIN + TS]).then_inc(dve_e.sem, dve_e.mark(("krot", l)))
                mul(m_k[0][rr, 0:TS], item("misc")[rr, 0:TS], con[rr, C_COS:C_COS + TS])
                for b in range(2):
                    V.tensor_copy(m_k[b][rr, TS:KEYS], small[rr, SM["kpe"]:SM["kpe"] + PAST])
                    ins = V.tensor_copy(m_k[b][rr, KEYS:KEYS + TP], item("misc")[rr, TS:T])
                ins.then_inc(dve_step.sem, dve_step.mark())
                dve.wait_ge(dve_step.sem, dve_step.n)
                dve.wait_ge(dve_e.sem, dve_e[("krot", l)])
                ttn(m_k[0][rr, 0:TS], m_k[0][rr, 0:TS], m_t[rr, 0:TS], ALU.add).then_inc(dve_step.sem, dve_step.mark())
                dve.wait_ge(dve_step.sem, dve_step.n)
                V.tensor_copy(m_k[1][rr, 0:TS], m_k[0][rr, 0:TS]).then_inc(dve_kpe.sem, dve_kpe.mark(l))

                def head_rot(h):
                    dve.wait_ge(act_e.sem, act_e[("mq", l, h)])
                    dve.wait_ge(filled.sem, filled[("qrot", l, h)])
                    at = place(("qrot", l, h))
                    mul(m_t[rr, 0:TS], psum[rr, at:at + TS], con[rr, C_SIN:C_SIN + TS]).then_inc(dve_e.sem, dve_e.mark(("qrot", l, h)))
                    mul(m_qr[h % 2][rr, :], m_qp[h % 2][rr, 0:TS], con[rr, C_COS:C_COS + TS]).then_inc(dve_step.sem, dve_step.mark())
                    dve.wait_ge(dve_step.sem, dve_step.n)
                    dve.wait_ge(dve_e.sem, dve_e[("qrot", l, h)])
                    ttn(m_qr[h % 2][rr, :], m_qr[h % 2][rr, :], m_t[rr, 0:TS], ALU.add).then_inc(dve_qr.sem, dve_qr.mark(l, h))
                    dve.wait_ge(dve_qr.sem, dve_qr[l, h])

                steps = [(h, i) for h in range(HEADS) for i in range(NT)]
                head_rot(0)
                for n in range(len(steps) + 2):
                    if n < len(steps):
                        h, i = steps[n]
                        if i == 3 and h + 1 < HEADS:
                            head_rot(h + 1)
                        w = KEYS if i < 4 else TP
                        dve.wait_ge(filled.sem, filled[("lg", l, h, i)])
                        at = place(("lg", l, h, i))
                        V.reduce_max(m_nm[:, n:n + 1], psum[:, at:at + w], AX.X, negate=True).then_inc(dve_nm.sem, dve_nm.mark(l, h, i))
                    if 1 <= n <= len(steps):
                        h, i = steps[n - 1]
                        w = KEYS if i < 4 else TP
                        dve.wait_ge(act_e.sem, act_e[("lg", l, h, i)])
                        V.reciprocal(m_rec[:, n - 1:n], m_sum[:, n - 1:n]).then_inc(dve_step.sem, dve_step.mark())
                        dve.wait_ge(dve_step.sem, dve_step.n)
                        ts(m_p[(n - 1) % 2][:, 0:w], m_p[(n - 1) % 2][:, 0:w], m_rec[:, n - 1:n]).then_inc(dve_pn.sem, dve_pn.mark(l, h, i))
                    if n >= 2:
                        h, i = steps[n - 2]
                        hs = slice(64 * (h % 2), 64 * (h % 2) + 64)
                        dve.wait_ge(filled.sem, filled[("mlaO", l, h, i)])
                        at = place(("mlaO", l, h, i))
                        o = item("mg", h // 2)[hs, P * i:P * i + P]
                        mul(o, o, psum[hs, at:at + P]).then_inc(dve_e.sem, dve_e.mark(("mlaO", l, h, i)))

                for n in range(KT):
                    dve.wait_ge(act_e.sem, act_e[("ma", l, n)])
                    dve.wait_ge(filled.sem, filled[("ya", l, n)])
                    at = place(("ya", l, n))
                    mul(yT[:, n, :], f_s[0], psum[:, at:at + T]).then_inc(dve_e.sem, dve_e.mark(("ya", l, n)))
                    dve.wait_ge(act_e.sem, act_e[("mb", l, n)])
                    dve.wait_ge(filled.sem, filled[("yb", l, n)])
                    at = place(("yb", l, n))
                    mul(f_t[0], f_s[1], psum[:, at:at + T]).then_inc(dve_e.sem, dve_e.mark(("yb", l, n)))
                    dve.wait_ge(dve_e.sem, dve_e[("yb", l, n)])
                    ttn(yT[:, n, :], yT[:, n, :], f_t[0], ALU.add).then_inc(dve_step.sem, dve_step.mark())
                    dve.wait_ge(dve_step.sem, dve_step.n)
                    dve.wait_ge(act_e.sem, act_e[("mc", l, n)])
                    dve.wait_ge(filled.sem, filled[("yc", l, n)])
                    at = place(("yc", l, n))
                    mul(f_t[1], f_s[2], psum[:, at:at + T]).then_inc(dve_e.sem, dve_e.mark(("yc", l, n)))
                    dve.wait_ge(dve_e.sem, dve_e[("yc", l, n)])
                    ttn(yT[:, n, :], yT[:, n, :], f_t[1], ALU.add).then_inc(dve_ysum.sem, dve_ysum.mark(l, n))
                    dve.wait_ge(dve_ysum.sem, dve_ysum[l, n])
                for n in range(KT):
                    dve.wait_ge(filled.sem, filled[("wo", l, n)])
                    at = place(("wo", l, n))
                    dve.wait_ge(s_xres[n % 2], 16 * (4 * l + n // 2 + 1))
                    stt3(hT[:, n, 0:TS], psum[:, at:at + TS], mod[:, 16 + n, 0:1], xres[n % 2][:, 0:TS],
                         ALU.mult, ALU.add)
                    ins = stt3(hT[:, n, TS:T], psum[:, at + TS:at + T], mod[:, 16 + n, 1:2], xres[n % 2][:, TS:T],
                               ALU.mult, ALU.add)
                    ins.then_inc(dve_e.sem, dve_e.mark(("wo", l, n)))
                dve.wait_ge(dve_e.sem, dve_e[("wo", l, KT - 1)])
            norm_input(DEPTH)
            dve.wait_ge(act_xrs.sem, act_xrs[DEPTH])
            for n in range(KT):
                stt3(acts[:, n, :], hT[:, n, :], v("final_g", n), w_rs, ALU.mult, ALU.mult).then_inc(dve_y.sem, dve_y.mark(n))
    return values


_FLOATS = {"xT": (P, KT, T), "units": (DEPTH, NU, P, UNIT), "small": (DEPTH, P, NSM), "vec": (DEPTH, P, NV),
           "con": (P, NC), "masks": (P, NM * 2 * P)}
_OUTS = {"yT": (P, KT, T), "new_ckv": (DEPTH, P, TP), "new_kpe": (DEPTH, 32, TP), "new_rw": (DEPTH, PAIRS, P, 2 * P),
         "new_gla": (DEPTH, P, 4 * P)}


def program(nc):
    a = {n: nc.dram_tensor(n, s, F32, kind="ExternalInput").ap() for n, s in _FLOATS.items()}
    for n, s in _OUTS.items():
        a[n] = nc.dram_tensor(n, s, F32, kind="ExternalOutput").ap()
    a["x_keep"] = nc.dram_tensor("x_keep", (P, KT, T), F32, kind="Internal").ap()
    return a


def lay_out(x):
    f = {n: np.asarray(w) for n, w in x.items()}
    tiles = lambda w: w.reshape(-1, P, w.shape[-1] // P, P).transpose(2, 1, 0, 3)
    cols = lambda w: w.reshape(-1, P).T
    out = {}
    tok = np.concatenate([f["x_sample"][0], f["x_prompt"][0]], 0)
    out["xT"] = tok.T.reshape(KT, P, T).transpose(1, 0, 2)
    units, small, vec = [], [], []
    off = {}
    at = 0
    for n, w in (("r", 512), ("k", 512), ("v", 512), ("wdad", 128), ("g", 512), ("gq", 256), ("gk", 256),
                 ("gv", 512), ("gad", 16), ("gg", 512), ("qd", 256), ("kvd", 128), ("kpe", 32), ("mg", 512),
                 ("ma", D), ("mb", D), ("mc", D)):
        off[n] = at
        at += w
    for l in range(DEPTH):
        w_in = f["w_in"][l].reshape(KT, P, -1)
        w_mod, w_out = tiles(f["w_mod"][l]), tiles(f["w_out"][l])
        o = {n: tiles(f[n][l]) for n in ("rw_out", "gla_out", "mla_out")}
        us = np.zeros((NU, P, KT, P), np.float32)
        for u, (n, i) in enumerate(UNITS):
            if n == "mod":
                us[u] = w_mod[i]
            elif n == "wo":
                us[u] = w_out[i]
            elif n == "oab":
                us[u, :, 0:4], us[u, :, 4:8] = o["rw_out"][i], o["gla_out"][i]
            elif n == "oc":
                us[u, :, 0:4] = o["mla_out"][i]
            elif n == "misc":
                us[u, :, :, 0:16] = w_in[:, :, off["gad"]:off["gad"] + 16].transpose(1, 0, 2)
                us[u, :, :, 64:96] = w_in[:, :, off["kpe"]:off["kpe"] + 32].transpose(1, 0, 2)
            else:
                us[u] = w_in[:, :, off[n] + P * i:off[n] + P * i + P].transpose(1, 0, 2)
        units.append(us.reshape(NU, P, UNIT))
        s = np.zeros((P, NSM), np.float32)
        s[0:64, SM["w2a2"]:SM["w2a2"] + 1024] = f["rw_w2"][l].transpose(1, 0, 2).reshape(64, 1024)
        s[64:128, SM["w2a2"]:SM["w2a2"] + 1024] = f["rw_a2"][l].transpose(1, 0, 2).reshape(64, 1024)
        s[0:16, SM["gla_a2"]:SM["gla_a2"] + 512] = f["gla_a2"][l].transpose(1, 0, 2).reshape(16, 512)
        s[:, SM["wq"]:SM["wq"] + 1536] = f["mla_wq_up"][l].reshape(2, P, 768).transpose(1, 0, 2).reshape(P, 1536)
        kv = f["mla_wkv_up"][l].reshape(P, HEADS, 2, 64)
        s[:, SM["wk"]:SM["wk"] + 512] = kv[:, :, 0].reshape(P, 512)
        s[:, SM["wv"]:SM["wv"] + 512] = kv[:, :, 1].reshape(P, 512)
        s[:, SM["ckv"]:SM["ckv"] + PAST] = f["cache_ckv"][0, l].T
        s[64:96, SM["kpe"]:SM["kpe"] + PAST] = f["cache_kpe"][0, l].T
        for d in range(2):
            for h in range(HEADS):
                c = SM["s_rw"] + P * (4 * d + h // 2) + 64 * (h % 2)
                s[64 * (h % 2):64 * (h % 2) + 64, c:c + 64] = f["state_rwkv"][0, l, d, h].T
            for h in range(4):
                c = SM["s_gla"] + P * (2 * d + h // 2)
                s[64 * (h % 2):64 * (h % 2) + 64, c:c + P] = f["state_gla"][0, l, d, h]
        small.append(s)
        cc = np.stack([cols(f["c"][0]), cols(f["c_ctx"])], -1).reshape(P, 16)
        vec.append(np.concatenate([cols(f["rw_w0"][l]), cols(f["rw_a0"][l]), cols(f["rw_k_k"][l]), cols(f["rw_k_a"][l]),
                                   cols(f["rw_r_k"][l]), cols(f["rw_ln_g"][l]), cols(f["rw_ln_b"][l]),
                                   cols(f["gla_ab"][l]), cols(f["gla_norm_g"][l]), cols(f["mla_qn_g"][l]),
                                   cols(f["mla_kvn_g"][l]), cols(f["norm_g"][l]), cols(f["b_mod"][l]), cc,
                                   cols(f["final_g"])], 1))
    out["units"], out["small"], out["vec"] = np.stack(units), np.stack(small), np.stack(vec)
    out["con"], out["masks"] = constant_table(), mask_table()
    return {n: np.ascontiguousarray(w) for n, w in out.items()}


def kernel(**inputs):
    import concourse.bacc as bacc
    from concourse.bass_utils import run_bass_kernel_spmd

    seen = {}
    for _ in range(2):
        nc = bacc.Bacc("TRN2", target_bir_lowering=False, num_devices=1)
        seen = build(nc, program(nc), seen)
    r = run_bass_kernel_spmd(nc, [lay_out(inputs)], core_ids=[0]).results[0]
    y = r["yT"].transpose(2, 1, 0).reshape(T, D)
    new_ckv = r["new_ckv"].transpose(0, 2, 1)[None]
    new_kpe = r["new_kpe"].transpose(0, 2, 1)[None]
    s = r["new_rw"].reshape(DEPTH, PAIRS, 2, 64, 2, 2, 64)
    rw = np.stack([s[:, :, h, :, :, h, :] for h in range(2)], 2)
    rw = rw.transpose(0, 4, 1, 2, 5, 3).reshape(DEPTH, 2, HEADS, 64, 64)[None]
    g = r["new_gla"].reshape(DEPTH, 2, 64, 2, 2, P).transpose(0, 4, 3, 1, 2, 5).reshape(DEPTH, 2, 4, 64, P)[None]
    return (np.ascontiguousarray(y[TS:])[None], np.ascontiguousarray(y[:TS])[None], np.ascontiguousarray(new_ckv),
            np.ascontiguousarray(new_kpe), np.ascontiguousarray(rw), np.ascontiguousarray(g))
```

```python
from contextlib import ExitStack

import numpy as np

import concourse.bass as bass
from concourse import mybir

F32 = mybir.dt.float32
U8 = mybir.dt.uint8
ACT = mybir.ActivationFunctionType
ALU = mybir.AluOpType
AX = mybir.AxisListType

P = 128
D = 1024
KT = D // P
TS, TP = 512, 128
T = TS + TP
NT = T // P
DEPTH = 2
PAST = 256
HEADS = 8
PAIRS = 4
GROUPS = ((0, 1), (2, 3), (4,))
LEVELS = (64, 32, 16, 8, 4, 2, 1)
SCALE = float(64 + 32) ** -0.5
KEYS = TS + PAST
DECAY = float(np.exp(-0.5))
RING = 5
UNIT = KT * P
NTMP = 8862 + 16 * 512

_names = (("w0", 8), ("a0", 8), ("k_k", 4), ("k_a", 4), ("r_k", 4), ("ln_g", 4), ("ln_b", 4), ("ab", 4),
          ("gla_g", 1), ("qn_g", 2), ("kvn_g", 1), ("norm_g", 8), ("b_mod", 24), ("c", 16), ("final_g", 8))
VEC, NV = {}, 0
for _n, _k in _names:
    VEC[_n] = NV
    NV += _k

_small = (("w2a2", 1024), ("gla_a2", 512), ("wq", 1536), ("wk", 512), ("wv", 512), ("ckv", PAST), ("kpe", PAST),
          ("s_rw", 8 * P), ("s_gla", 4 * P))
SM, NSM = {}, 0
for _n, _k in _small:
    SM[_n] = NSM
    NSM += _k

ALL_REST = ([("misc", 0)] + [("gq", i) for i in range(2)] + [("gk", i) for i in range(2)]
              + [("gv", i) for i in range(4)] + [("gg", i) for i in range(4)]
              + [("qd", i) for i in range(2)] + [("kvd", 0)] + [("mg", i) for i in range(4)])
FIRST_ITEMS = [("wdad", 0), ("k", 0), ("r", 0), ("v", 0)]
BESIDE = [[("k", 1), ("r", 1), ("v", 1), ("g", 0)], [("v", 2), ("k", 3), ("r", 3), ("g", 1)],
          [("gq", 0), ("gq", 1), ("gk", 0), ("g", 2)], [("gv", 1), ("gv", 2), ("gv", 3), ("g", 3)]]
BESIDE_PROMPT = [[("k", 2), ("r", 2)], [("v", 3), ("misc", 0)], [("gk", 1), ("gv", 0)], [("qd", 0), ("qd", 1)]]
END_ITEMS = [("kvd", 0)]
REST_ITEMS = [("gg", 0)]
GLA_KEYS = {(0, 0): ("gg", 1), (0, 1): ("mg", 0), (1, 0): ("mg", 1), (1, 1): ("mg", 2)}
GLA_LEVEL = {(0, 0): ("gg", 2), (0, 1): ("gg", 3), (1, 0): ("mg", 3), (1, 1): ("ma", 4)}
MLA_MERGE = [("ma", n) for n in (0, 1, 2, 3, 5, 6, 7)]
MERGE_AT = 3
MOD_GROUPS = 6
ROUNDS = MOD_GROUPS * KT // PAIRS


def unit_order(l):
    order = [(l, it) for it in FIRST_ITEMS]
    for p in range(PAIRS):
        order += [(l, it) for it in BESIDE[p]]
        beside = []
        if l + 1 < DEPTH:
            beside += [(2 * i, (l + 1, ("mod", ROUNDS // 2 * p + i))) for i in range(ROUNDS // 2)]
        beside += [(6 * i + 0.5, (l, it)) for i, it in enumerate(BESIDE_PROMPT[p])]
        order += [u for _, u in sorted(beside)]
    order += [(l, it) for it in END_ITEMS + REST_ITEMS]
    order += [(l, it[pd]) for pd in GLA_KEYS for it in (GLA_KEYS, GLA_LEVEL) if pd in it]
    order += [(l, it) for it in MLA_MERGE]
    order += [(l, (u, n)) for n in range(8) for u in ("oab", "mb", "mc", "oc")]
    return order + [(l, ("wo", n)) for n in range(8)]


STREAM = [(0, ("mod", i)) for i in range(24)] + [u for _l in range(DEPTH) for u in unit_order(_l)]
UNITS = [("mod", i) for i in range(24)] + [u for _l, u in unit_order(DEPTH - 1)]
NU = len(UNITS)
SLOT = {("g", i): i for i in range(4)}
SLOT.update({(n, i): 4 + 3 * i + j for i in range(4) for j, n in enumerate("krv")})
SLOT[("wdad", 0)] = 16
SLOT.update({it: 4 + j for j, it in enumerate(ALL_REST)})
SLOT_MERGE = SLOT["gq", 0]
SLOT.update({("ma", n): SLOT_MERGE + n for n in range(8)})
GATES = ("g", "gg", "mg")

M_X, M_XT, M_OFF, M_INC, M_STR, M_LEVEL, M_ID = 0, 1, 2, 3, 4, 5, 12
NM = 13


def mask_table():
    s, t = np.meshgrid(np.arange(P), np.arange(P), indexing="ij")
    m = np.zeros((P, NM, 2, P), np.float32)
    same = (s ^ t) < 16
    for d in range(2):
        before = (s < t) if d == 0 else (s > t)
        after = (s > t) if d == 0 else (s < t)
        m[:, M_XT, d] = before & same
        m[:, M_X, d] = after & same
        m[:, M_OFF, d] = after & ~same
        m[:, M_INC, d] = before | (s == t)
        m[:, M_STR, d] = before
        for j, h in enumerate(LEVELS):
            m[:, M_LEVEL + j, d] = before & ((s ^ t) >= h) & ((s ^ t) < 2 * h)
        m[:, M_ID, d] = s == t
    return m.reshape(P, -1)


C_ID, C_ONES, C_BD, C_ROT, C_COS, C_SIN, C_BIAS = 0, 128, 256, 384, 416, 928, 1440
NC = 1448


def constant_table():
    c = np.zeros((P, NC), np.float32)
    c[:, C_ID:C_ID + P] = np.eye(P)
    c[:, C_ONES:C_ONES + P] = 1.0
    c[:, C_BD:C_BD + P] = np.kron(np.eye(2), np.ones((64, 64)))
    n_freq = 8
    inv = np.float32(10000.0) ** (-np.arange(n_freq, dtype=np.float32) / np.float32(n_freq))
    pos = [np.arange(TS) // 64, np.arange(TS) % 64]
    for r in range(32):
        axis, half, f = r // 16, r // 8 % 2, r % 8
        ang = (pos[axis].astype(np.float32) * inv[f]).astype(np.float32)
        c[64 + r, C_COS:C_COS + TS] = np.cos(ang)
        c[64 + r, C_SIN:C_SIN + TS] = np.sin(ang) * (-1.0 if half == 0 else 1.0)
        c[64 + r, C_ROT + (r ^ 8)] = 1.0
    for j, b in enumerate((1e-6, 64e-5, 0.5 * 20 * np.log(2.0), 1.0)):
        c[:, C_BIAS + j] = b
    return c


class Signal:

    def __init__(self, sem, name, values, seen):
        self.sem, self.name, self.values, self.seen, self.n = sem, name, values, seen, 0

    def mark(self, *key):
        self.n += 1
        self.values[self.name, key[0] if len(key) == 1 else key] = self.n
        return 1

    def __getitem__(self, key):
        return self.seen.get((self.name, key), 1)


def build(nc, a, seen):
    values = {}
    ctx = ExitStack()
    with ctx:
        def sb(name, shape, dt=F32):
            return ctx.enter_context(nc.sbuf_tensor(name, shape, dt))

        def sem(name):
            return ctx.enter_context(nc.semaphore(name))

        def signal(name):
            return Signal(sem(name), name, values, seen)

        psum = ctx.enter_context(nc.psum_tensor("psum", [P, 8 * 512], F32))
        hT = sb("hT", [P, KT, T])
        ring = sb("ring", [P, RING, UNIT])
        small = sb("small_sb", [P, NSM])
        vec = sb("vec_sb", [P, NV])
        con = sb("con_sb", [P, NC])
        masks = sb("masks_sb", [P, NM, 2, P], U8)
        acts = sb("acts", [P, 24, T])
        gate = sb("gate", [P, T])
        sc = sb("sc", [P, KT, 2])
        sc_t = sb("sc_t", [P, KT, 2])
        mod = sb("mod", [P, 24, 2])
        mod_new = sb("mod_new", [P, 24, 2])
        gs = sb("gs", [P, KT, 2])
        omka = sb("omka", [P, 4])
        tmp = sb("tmp", [P, NTMP])

        ident = con[:, C_ID:C_ID + P]
        ones = con[:, C_ONES:C_ONES + P]
        bd = con[:, C_BD:C_BD + P]

        def mod_row(j):
            return con[0:2, C_COS + 512 * (j % 2):C_COS + 512 * (j % 2) + 512]

        def v(name, i=0, p=slice(0, P)):
            return vec[p, VEC[name] + i:VEC[name] + i + 1]

        def item(name, i=0):
            return acts[:, SLOT[name, i], :]

        def area(at, *shape):
            n = int(np.prod(shape))
            assert at + n <= NTMP, (at, shape)
            x = tmp[:, at:at + n]
            if len(shape) == 2:
                x = x.rearrange("p (a b) -> p a b", a=shape[0])
            elif len(shape) == 3:
                x = x.rearrange("p (a b c) -> p a b c", a=shape[0], b=shape[1])
            return x
        fac = area(0, 8, T)
        A_, R_, B_, K_ = range(4)
        w_kk, w_sw, w_ys, w_a, w_e = (area(5120 + T * j, T) for j in range(5))
        stt = area(8320, 2, 2, NT)
        trn = area(8340, 2, NT)
        st = area(8350, 2, P)
        st_t = area(8606, 2, P)
        NAMES = ["XT", "X", "Off", "AakT", "ArbT", "ArkT", "G", "H", "I", "J", "K", "TB", "TA"]

        def gbuf(g, name):
            k = NAMES.index(name)
            if g == 0:
                return area(8862 + 512 * k, 4, P)
            if k < 3:
                return area(8862 + 512 * (13 + k), 4, P)
            rest = acts[:, 17:24, :].rearrange("p a b -> p (a b)")
            if k < 11:
                o = 512 * (k - 3)
                return rest[:, o:o + 512].rearrange("p (a b) -> p a b", a=4)
            o = 512 * (k - 11)
            return gate2[:, o:o + 512].rearrange("p (a b) -> p a b", a=4)
        gate2 = sb("gate2", [P, 1024])
        sraw = sb("sraw", [P, 2, 2, NT])

        w_rs = area(0, T)
        g_qi = [area(0, T), area(640, T)]
        g_ki = area(1280, T)
        g_kit = area(1920, NT, P)
        g_vt = area(2560, 10, P)
        g_st = [area(3840, NT, P), area(4480, NT, P)]
        g_att = [area(5120, 10, P), area(6400, 10, P)]
        g_kl = [area(7680, T), area(8320, T)]
        g_ql = [area(8960, T), area(9600, T)]
        g_b, g_z = area(10240, T), area(10880, T)
        g_e = [area(11520, T), area(12160, T)]
        g_d, g_x, g_ax = area(12800, T), area(13440, T), area(14080, T)
        g_eq, g_ek = g_e
        g_osq, g_o = area(14720, T), area(15360, T)
        g_new = area(16000, 4, P)
        g_dec = sb("g_dec", [P, NT])

        def halves(d):
            a, b = slice(0, 64), slice(64, 128)
            return (a, b) if d == 0 else (b, a)
        g_osqs, g_os, g_rs = [g_osq, g_d], [g_o, g_x], [g_ax, g_z]
        m_sq = [area(T * j, T) for j in range(3)]
        m_k = [area(1920, KEYS + TP), area(2816, KEYS + TP)]
        m_qp = [area(3712, T), area(4352, T)]
        m_qr = [area(4992, TS), area(5504, TS)]
        m_v = area(6016, 7, 512)
        m_p = [area(9600, KEYS), area(10368, KEYS), area(14592, KEYS)]
        m_pt = [area(11136, KEYS), area(11904, KEYS)]
        m_t = area(12672, T)
        m_r = [area(13312, T), area(13952, T)]
        m_nm, m_sum, m_rec = (sb(n, [P, HEADS * NT]) for n in ("m_nm", "m_sum", "m_rec"))
        yT = area(0, KT, T)
        xres = [area(5120, T), area(5760, T)]
        f_s = [area(14400 + T * j, T) for j in range(3)]
        f_t = [area(12672, T), area(16320, T)]

        s_con = sem("constants_loaded")
        s_masks = sem("masks_loaded")
        s_vec = sem("layer_vectors_loaded")
        s_small = sem("layer_weights_loaded")
        s_x = sem("x_loaded")
        s_unit = [sem(f"unit{j}_loaded") for j in range(RING)]
        s_out = sem("outputs_written")
        s_sto = sem("states_written")
        s_gst = sem("gla_states_written")
        s_keep = sem("x_kept")
        s_xres = [sem(f"x_reloaded{j}") for j in range(2)]
        filled = signal("psum_filled")
        act_e = signal("act_emptied")
        dve_e = signal("dve_emptied")
        used = signal("unit_used")
        act_step = signal("act_step")
        dve_step = signal("dve_step")
        act_J = signal("act_J")
        act_ex = signal("act_ex")
        act_gexp = signal("act_gexp")
        act_gln = signal("act_gln")
        act_grs = signal("act_grs")
        act_kvrs = signal("act_kvrs")
        act_le = signal("act_le")
        act_ors = signal("act_ors")
        act_qrs = signal("act_qrs")
        act_rn = signal("act_rn")
        act_sc = signal("act_sc")
        act_sig = signal("act_sig")
        act_tanh = signal("act_tanh")
        act_xrs = signal("act_xrs")
        dve_FT = signal("dve_FT")
        dve_MT1 = signal("dve_MT1")
        dve_ckv = signal("dve_ckv")
        dve_fac = signal("dve_fac")
        dve_gax = signal("dve_gax")
        dve_gla_out = signal("dve_gla_out")
        dve_gosq = signal("dve_gosq")
        dve_gstates = signal("dve_gstates")
        dve_gz = signal("dve_gz")
        act_h = signal("act_h")
        act_ma = signal("act_ma")
        act_ta = signal("act_ta")
        dve_h = signal("dve_h")
        dve_xn = signal("dve_xn")
        dve_ki = signal("dve_ki")
        dve_kksq = signal("dve_kksq")
        dve_kpe = signal("dve_kpe")
        dve_kq = signal("dve_kq")
        dve_kvsq = signal("dve_kvsq")
        dve_lvl = signal("dve_lvl")
        dve_new_state = signal("dve_new_state")
        dve_nm = signal("dve_nm")
        dve_osq = signal("dve_osq")
        dve_pn = signal("dve_pn")
        dve_qn = signal("dve_qn")
        dve_qr = signal("dve_qr")
        dve_qsq = signal("dve_qsq")
        dve_rkr = signal("dve_rkr")
        dve_rwkv_done = signal("dve_rwkv_done")
        dve_sc = signal("dve_sc")
        dve_state = signal("dve_state")
        dve_state_done = signal("dve_state_done")
        dve_xsq = signal("dve_xsq")
        dve_y = signal("dve_y")
        dve_ysum = signal("dve_ysum")
        dve_yz = signal("dve_yz")
        dve_zeroed = signal("dve_zeroed")
        pool_g1 = signal("pool_g1")
        pool_gate = signal("pool_gate")
        pool_gla_stored = signal("pool_gla_stored")
        emptied = {"act": act_e, "dve": dve_e}

        book = {"at": 0, "last": [None] * 8, "held": set()}

        def ticket(pe, key, banks, by):
            at = book["at"]
            while at + banks > 8 or any(b in book["held"] for b in range(at, at + banks)):
                at = (at + 1) % 8
            for old, o_by in dict.fromkeys(o for o in book["last"][at:at + banks] if o):
                pe.wait_ge(emptied[o_by].sem, emptied[o_by][old])
            book["last"][at:at + banks] = [(key, by)] * banks
            book["at"] = (at + banks) % 8
            values["at", key] = at
            return at * 512

        def place(key):
            return seen.get(("at", key), 0) * 512

        block = ctx.enter_context(nc.Block())

        @block.sync
        def _(sp):
            sp.dma_start(vec[:, :], a["vec"][0]).then_inc(s_vec, 16)
            for n, (l, (name, i)) in enumerate(STREAM):
                if n == 1:
                    sp.dma_start(con[:, :], a["con"]).then_inc(s_con, 16)
                if n == 4 * RING:
                    sp.dma_start(area(5120, NM * 2 * P), a["masks"]).then_inc(s_masks, 16)
                if l and (name, i) == FIRST_ITEMS[0]:
                    sp.wait_ge(dve_e.sem, dve_e[("mlaO", l - 1, 7, 4)])
                    sp.dma_start(vec[:, :], a["vec"][l]).then_inc(s_vec, 16)
                if n >= RING:
                    ol, (old, oi) = STREAM[n - RING]
                    if old == "mod" and oi % 4 < 3:
                        sp.wait_ge(used.sem, used[(ol, oi)])
                    elif old == "mod":
                        sp.wait_ge(filled.sem, filled[("modrow", ol, oi // 4)])
                    elif (old, oi) in SLOT:
                        sp.wait_ge(filled.sem, filled[(ol, old, oi)])
                    else:
                        sp.wait_ge(filled.sem, filled[({"oab": "yb", "oc": "yc"}.get(old, old), ol, oi)])
                sp.dma_start(ring[:, n % RING, :], a["units"][l, UNITS.index((name, i))]).then_inc(s_unit[n % RING], 16)

        @block.gpsimd
        def _(pool):
            for l in range(DEPTH):
                if l == 0:
                    pool.wait_ge(filled.sem, filled[("modrow", 0, 0)])
                    pool.dma_start(hT[:, :, :], a["xT"]).then_inc(s_x, 16)
                    pool.wait_ge(filled.sem, filled[("modrow", 0, 4)])
                    pool.dma_start(small[:, :], a["small"][l]).then_inc(s_small, 16)
                    pool.memset(gate[:, :], 1.0)
                    pool.memset(gate2[:, :], 0.0).then_inc(pool_g1.sem, pool_g1.mark(0))
                    pool.wait_ge(pool_g1.sem, pool_g1[0])
                    pool.wait_ge(s_masks, 16)
                    pool.tensor_copy(masks[:, :, :, :].rearrange("p a b c -> p (a b c)"), area(5120, NM * 2 * P))
                    pool.memset(gate[:, ::P], 0.0).then_inc(pool_gate.sem, pool_gate.mark(0))
                for p in range(PAIRS):
                    pool.wait_ge(dve_new_state.sem, dve_new_state[l, p])
                    pool.dma_start(a["new_rw"][l, p], st_t.rearrange("p a b -> p (a b)")).then_inc(s_sto, 16)
                for p in range(2):
                    for d in range(2):
                        pool.wait_ge(dve_e.sem, dve_e[("gs", l, p, d)])
                pool.dma_start(a["new_gla"][l], g_new.rearrange("p a b -> p (a b)")).then_inc(s_gst, 16)
                pool.wait_ge(s_gst, 16 * (l + 1))
                pool.memset(gate2[:, 0:1], 0.0).then_inc(pool_gla_stored.sem, pool_gla_stored.mark(l))
                pool.wait_ge(act_e.sem, act_e[(l, "misc", 0)])
                pool.dma_start(a["new_kpe"][l], item("misc")[64:96, TS:T]).then_inc(s_out, 16)
                pool.wait_ge(dve_ckv.sem, dve_ckv[l])
                pool.dma_start(a["new_ckv"][l], item("kvd")[:, TS:T]).then_inc(s_out, 16)
                pool.wait_ge(dve_e.sem, dve_e[("mlaO", l, 7, 4)])
                if l + 1 < DEPTH:
                    pool.wait_ge(filled.sem, filled[("mlaO", l, 7, 4)])
                    pool.dma_start(small[:, :], a["small"][l + 1]).then_inc(s_small, 16)
                x_old = a["xT"] if l == 0 else a["x_keep"]
                for n in range(KT):
                    if n >= 2:
                        pool.wait_ge(dve_e.sem, dve_e[("wo", l, n - 2)])
                    pool.dma_start(xres[n % 2], x_old[:, n, :]).then_inc(s_xres[n % 2], 16)
                    if l == 0 and n >= 2:
                        pool.dma_start(a["x_keep"][:, n - 2, :], hT[:, n - 2, :]).then_inc(s_keep, 16)
                if l == 0:
                    for n in (KT - 2, KT - 1):
                        pool.wait_ge(dve_e.sem, dve_e[("wo", l, n)])
                        pool.dma_start(a["x_keep"][:, n, :], hT[:, n, :]).then_inc(s_keep, 16)
            for n in range(KT):
                pool.wait_ge(dve_y.sem, dve_y[n])
                pool.dma_start(a["yT"][:, n, :], acts[:, n, :]).then_inc(s_out, 16)
            pool.wait_ge(s_out, 16 * (2 * DEPTH + KT))
            pool.wait_ge(s_sto, 16 * DEPTH * PAIRS)
            pool.wait_ge(s_keep, 16 * KT)

        @block.tensor
        def _(pe):
            def mm(out, lhsT, rhs, start, stop):
                return nc.tensor.matmul(out, lhsT, rhs, start=start, stop=stop, skip_group_check=True)

            def tr(out, in_, p=P):
                return nc.tensor.transpose(out, in_, ident[0:p, 0:p])

            def wide(at, lhsT, rhs, start=True, stop=True, m=slice(0, P)):
                mm(psum[m, at:at + TS], lhsT, rhs[:, 0:TS], start, stop)
                return mm(psum[m, at + TS:at + T], lhsT, rhs[:, TS:T], start, stop)

            count = [0]

            def unit(k=KT):
                n = count[0]
                pe.wait_ge(s_unit[n % RING], 16 * (n // RING + 1))
                return ring[:, n % RING, :].rearrange("p (k n) -> p k n", k=k)

            def unit_done():
                count[0] += 1

            def project(l, it):
                w = unit()
                key = (l, *it)
                at = ticket(pe, key, 2, "dve" if it[0] in GATES else "act")
                for k in range(KT):
                    if it == FIRST_ITEMS[0]:
                        pe.wait_ge(act_h.sem, act_h[l, k])
                        pe.wait_ge(dve_h.sem, dve_h[l, k])
                    mm(psum[:, at:at + TS], w[:, k, :], hT[:, k, 0:TS], k == 0, k == KT - 1)
                for k in range(KT):
                    last = mm(psum[:, at + TS:at + T], w[:, k, :], hT[:, k, TS:T], k == 0, k == KT - 1)
                last.then_inc(filled.sem, filled.mark(key))
                unit_done()

            def sums(key, lhsT, rhs_list, by="act"):
                at = ticket(pe, key, 2, by)
                for j, r in enumerate(rhs_list):
                    last = wide(at, lhsT, r, j == 0, j == len(rhs_list) - 1)
                last.then_inc(filled.sem, filled.mark(key))

            grown = {}

            def mod_product(l, j, k):
                if k == 0:
                    grown["at"] = ticket(pe, ("modrow", l, j), 1, "act")
                    book["held"].add(grown["at"] // 512)
                if k % 2 == 0:
                    grown["w"] = unit(2)
                    unit_done()
                at = grown["at"]
                last = mm(psum[0:2, at:at + 512], sc[:, k, :], grown["w"][:, k % 2, :], k == 0, k == KT - 1)
                if k == KT - 1:
                    last.then_inc(filled.sem, filled.mark(("modrow", l, j)))
                    book["held"].discard(at // 512)
                elif k % 2 == 1:
                    last.then_inc(used.sem, used.mark((l, 4 * j + k // 2)))

            def project_some(l, it, tiles):
                key = (l, *it)
                for k in tiles:
                    if k == 0:
                        grown["item_at"] = ticket(pe, key, 2, "act")
                        book["held"] |= {grown["item_at"] // 512, grown["item_at"] // 512 + 1}
                        grown["item_w"] = unit()
                        unit_done()
                    at = grown["item_at"]
                    last = wide(at, grown["item_w"][:, k, :], hT[:, k, :], k == 0, k == KT - 1)
                    if k == KT - 1:
                        last.then_inc(filled.sem, filled.mark(key))
                        book["held"] -= {at // 512, at // 512 + 1}

            def mod_turn(l, j):
                pe.wait_ge(act_e.sem, act_e[("modrow", l, j)])
                at = ticket(pe, ("mod", l, j), 1, "dve")
                for i in range(4):
                    last = tr(psum[:, at + 2 * i:at + 2 * i + 2], mod_row(j)[:, P * i:P * i + P], 2)
                last.then_inc(filled.sem, filled.mark(("mod", l, j)))

            def mean_square(l):
                at = ticket(pe, ("xss", l), 2, "act")
                for k in range(KT):
                    pe.wait_ge(dve_xsq.sem, dve_xsq[l, k])
                    last = wide(at, ones, acts[:, k, :], k == 0, k == KT - 1)
                last.then_inc(filled.sem, filled.mark(("xss", l)))

            pe.wait_ge(dve_sc.sem, dve_sc[0])
            for j in range(MOD_GROUPS):
                for k in range(KT):
                    mod_product(0, j, k)
                if j == 0:
                    pe.wait_ge(s_con, 16)
                else:
                    mod_turn(0, j - 1)
                if j == MOD_GROUPS - 2:
                    mean_square(0)
            mod_turn(0, MOD_GROUPS - 1)

            for l in range(DEPTH):
                if l:
                    mean_square(l)
                for it in FIRST_ITEMS:
                    project(l, it)

                pe.wait_ge(s_small, 16 * (l + 1))
                pe.wait_ge(act_e.sem, act_e[(l, "wdad", 0)])
                pe.wait_ge(act_tanh.sem, act_tanh[l])
                for p in range(PAIRS):
                    project(l, BESIDE[p][0])
                    pe.wait_ge(dve_kksq.sem, dve_kksq[l, p])
                    sums(("kkss", l, p), bd, [w_ys], by="dve")
                    for d in range(2):
                        for n, rows in (("zw", slice(0, 64)), ("za", slice(64, 128))):
                            at = ticket(pe, (n, l, p, d), 2, "act")
                            w = small[rows, SM["w2a2"] + 512 * d + P * p:SM["w2a2"] + 512 * d + P * p + P]
                            wide(at, w, item("wdad")[rows, :]).then_inc(filled.sem, filled.mark((n, l, p, d)))
                        for it in BESIDE[p][1:2] if d == 0 else BESIDE[p][2:4]:
                            project(l, it)
                    for d in range(2):
                        pe.wait_ge(dve_fac.sem, dve_fac[l, p, d])
                    for steps in GROUPS:
                        def beat(r):
                            if steps == (4,) and l + 1 < DEPTH:
                                j, k = divmod(ROUNDS * p + r, KT)
                                mod_product(l + 1, j, k)
                                if k == 2 and j:
                                    mod_turn(l + 1, j - 1)
                            if steps == (4,) and BESIDE_PROMPT[p]:
                                n = 8 * r // 6
                                project_some(l, BESIDE_PROMPT[p][r // 6], range(n % KT, 8 * (r + 1) // 6 - n + n % KT))

                        def tile(d, s):
                            return s if s == 4 or d == 0 else 3 - s

                        def cols(d, s):
                            return slice(P * tile(d, s), P * tile(d, s) + P)

                        def F(d, kind, s):
                            return fac[:, 4 * d + kind, cols(d, s)]

                        def units():
                            return [(u, u // 2, slice(64 * (u % 2), 64 * (u % 2) + 64)) for u in range(4)]

                        def each(s, key, by, f):
                            at = ticket(pe, (key, l, p, s), 1, by)
                            for u in range(4):
                                lhsT, rhs = f(u)
                                last = mm(psum[:, at + P * u:at + P * u + P], lhsT, rhs, True, True)
                            last.then_inc(filled.sem, filled.mark((key, l, p, s)))

                        def got(s, *keys):
                            for key, by in keys:
                                pe.wait_ge(emptied[by].sem, emptied[by][(key, l, p, s)])

                        for s in steps:
                            at = ticket(pe, ("TB", l, p, s), 1, "act")
                            for d in range(2):
                                tr(psum[:, at + 256 * d:at + 256 * d + P], F(d, B_, s))
                                last = tr(psum[:, at + 256 * d + P:at + 256 * d + 256], F(d, K_, s))
                            last.then_inc(filled.sem, filled.mark(("TB", l, p, s)))
                            at = ticket(pe, ("TA", l, p, s), 1, "act")
                            for d in range(2):
                                tr(psum[:, at + 256 * d:at + 256 * d + P], F(d, A_, s))
                                last = tr(psum[:, at + 256 * d + P:at + 256 * d + 256], item("v", p)[:, cols(d, s)])
                            last.then_inc(filled.sem, filled.mark(("TA", l, p, s)))
                        for s in steps:
                            for key, kind, rhs in (("Ab", B_, (A_, R_)), ("Ak", K_, (A_, R_)), ("Aab", A_, (B_, B_))):
                                at = ticket(pe, (key, l, p, s), 2, "dve")
                                n = rhs[1] - rhs[0] + 1
                                for d in range(2):
                                    moving = fac[:, 4 * d + rhs[0]:4 * d + rhs[1] + 1, cols(d, s)]
                                    for h in range(2):
                                        hs = slice(64 * h, 64 * h + 64)
                                        o = at + 512 * h + 256 * d
                                        last = mm(psum[:, o:o + P * n], F(d, kind, s)[hs, :], moving[hs], True, True)
                                last.then_inc(filled.sem, filled.mark((key, l, p, s)))

                        def B(s, name):
                            g = gbuf(s % 2, name)
                            return lambda u: g[:, u, :]
                        beat(0)
                        for s in steps:
                            got(s, ("Ab", "dve"), ("Aab", "dve"))
                            each(s, "X2", "act", lambda u: (B(s, "XT")(u), B(s, "X")(u)))
                            each(s, "X2T", "act", lambda u: (B(s, "X")(u), B(s, "XT")(u)))
                        beat(1)
                        for s in steps:
                            got(s, ("X2", "act"), ("X2T", "act"))
                            pe.wait_ge(dve_FT.sem, dve_FT[l, p, s])
                            each(s, "X4", "act", lambda u: (B(s, "I")(u), B(s, "H")(u)))
                            each(s, "X4T", "act", lambda u: (B(s, "H")(u), B(s, "I")(u)))
                            each(s, "GT", "dve", lambda u: (B(s, "H")(u), B(s, "G")(u)))
                        beat(2)
                        for s in steps:
                            got(s, ("X4", "act"), ("X4T", "act"), ("GT", "dve"))
                            each(s, "X8", "act", lambda u: (B(s, "XT")(u), B(s, "X")(u)))
                            each(s, "HT", "dve", lambda u: (B(s, "X")(u), B(s, "G")(u)))
                        beat(3)
                        for s in steps:
                            got(s, ("X8", "act"), ("HT", "dve"))
                            each(s, "T16T", "dve", lambda u: (B(s, "H")(u), B(s, "G")(u)))
                        beat(4)
                        for s in steps:
                            got(s, ("T16T", "dve"), ("Ak", "dve"), ("TA", "act"))
                            each(s, "NT", "act", lambda u: (B(s, "Off")(u), B(s, "G")(u)))
                            each(s, "N", "act", lambda u: (B(s, "G")(u), B(s, "Off")(u)))
                            at = ticket(pe, ("AV", l, p, s), 1, "act")
                            for u in range(4):
                                d, h = u // 2, u % 2
                                last = mm(psum[:, at + 64 * u:at + 64 * u + 64], B(s, "AakT")(u),
                                          gbuf(s % 2, "TA")[:, 2 * d + 1, 64 * h:64 * h + 64], True, True)
                            last.then_inc(filled.sem, filled.mark(("AV", l, p, s)))
                        beat(5)
                        for s in steps:
                            got(s, ("NT", "act"), ("N", "act"), ("AV", "act"))
                            each(s, "N2", "act", lambda u: (B(s, "I")(u), B(s, "H")(u)))
                            each(s, "N2T", "act", lambda u: (B(s, "H")(u), B(s, "I")(u)))
                            pe.wait_ge(act_J.sem, act_J[l, p, s])
                            each(s, "Y1", "dve", lambda u: (B(s, "G")(u), B(s, "J")(u)))
                        beat(6)
                        for s in steps:
                            got(s, ("N2", "act"), ("N2T", "act"))
                            pe.wait_ge(dve_MT1.sem, dve_MT1[l, p, s])
                            each(s, "N4", "act", lambda u: (B(s, "AakT")(u), B(s, "Off")(u)))
                            each(s, "MT2", "dve", lambda u: (B(s, "Off")(u), B(s, "I")(u)))
                        beat(7)
                        for s in steps:
                            got(s, ("N4", "act"), ("MT2", "dve"))
                            each(s, "MT3", "dve", lambda u: (B(s, "H")(u), B(s, "I")(u)))
                        beat(8)
                        for s in steps:
                            got(s, ("MT3", "dve"), ("Y1", "dve"))
                            each(s, "Y", "act", lambda u: (B(s, "I")(u), B(s, "K")(u)))
                        beat(9)
                        for s in steps:
                            pe.wait_ge(act_ta.sem, act_ta[l, p, s])
                            at = ticket(pe, ("TaT", l, p, s), 1, "act")
                            for d in range(2):
                                last = tr(psum[:, at + P * d:at + P * d + P], gbuf(s % 2, "J")[:, d, :])
                            last.then_inc(filled.sem, filled.mark(("TaT", l, p, s)))
                        beat(10)
                        for s in steps:
                            K, TA, TB = gbuf(s % 2, "K"), gbuf(s % 2, "TA"), gbuf(s % 2, "TB")
                            got(s, ("TB", "act"))
                            s_at = ticket(pe, ("S", l, p, s), 1, "dve") if s != 3 else None
                            for d in range(2) if s != 3 else ():
                                mm(psum[:, s_at + P * d:s_at + P * d + P], TB[:, 2 * d + 1, :],
                                   TA[:, 2 * d + 1, :], d == 0, False)
                            at = ticket(pe, ("O", l, p, s), 1, "dve")
                            for u in range(4):
                                d, hs = u // 2, slice(64 * (u % 2), 64 * (u % 2) + 64)
                                mm(psum[hs, at + P * d:at + P * d + P], TA[:, 2 * d + 1, hs], B(s, "ArkT")(u),
                                   d == 0, False)
                            got(s, ("TaT", "act"))
                            pe.wait_ge(dve_state.sem, dve_state[l, p, s])
                            u_at = ticket(pe, ("U", l, p, s), 1, "dve")
                            for d in range(2):
                                last = mm(psum[:, u_at + P * d:u_at + P * d + P], K[:, d, :], st[:, d, :], True, True)
                            last.then_inc(filled.sem, filled.mark(("U", l, p, s)))
                            for d in range(2):
                                mm(psum[:, at + P * d:at + P * d + P], st[:, d, :], F(d, R_, s), False, False)
                            got(s, ("U", "dve"))
                            for d in range(2) if s != 3 else ():
                                last = mm(psum[:, s_at + P * d:s_at + P * d + P], TB[:, 2 * d, :], K[:, 2 + d, :],
                                          False, True)
                            if s != 3:
                                last.then_inc(filled.sem, filled.mark(("S", l, p, s)))
                            for d in range(2):
                                for h in range(2):
                                    u, hs = 2 * d + h, slice(64 * h, 64 * h + 64)
                                    last = mm(psum[hs, at + P * d:at + P * d + P], K[:, 2 + d, hs], B(s, "ArbT")(u),
                                              False, True)
                            last.then_inc(filled.sem, filled.mark(("O", l, p, s)))
                    pe.wait_ge(dve_rkr.sem, dve_rkr[l, p])
                    sums(("bonus", l, p), bd, [item("r", p)], by="dve")
                    pe.wait_ge(dve_e.sem, dve_e[("O", l, p, 4)])
                    sums(("omean", l, p), bd, [item("k", p)], by="dve")
                    beat(11)
                    pe.wait_ge(dve_osq.sem, dve_osq[l, p])
                    sums(("ovar", l, p), bd, [w_ys], by="act")
                if l + 1 < DEPTH:
                    mod_turn(l + 1, MOD_GROUPS - 1)
                for it in END_ITEMS:
                    project(l, it)

                for it in REST_ITEMS:
                    pe.wait_ge(dve_rwkv_done.sem, dve_rwkv_done[l])
                    project(l, it)

                for p in range(2):
                    pe.wait_ge(act_e.sem, act_e[(l, "gv", 2 * p + 1)])
                    for h in range(2):
                        at = ticket(pe, ("gvt", l, p, h), 2, "act")
                        for i in range(NT):
                            last = tr(psum[:, at + P * i:at + P * i + P], item("gv", 2 * p + h)[:, P * i:P * i + P])
                        last.then_inc(filled.sem, filled.mark(("gvt", l, p, h)))
                    for d in range(2):
                        at = ticket(pe, ("gx", l, p, d), 2, "dve")
                        w = small[0:16, SM["gla_a2"] + 256 * d + P * p:SM["gla_a2"] + 256 * d + P * p + P]
                        wide(at, w, item("misc")[0:16, :]).then_inc(filled.sem, filled.mark(("gx", l, p, d)))
                        project(l, GLA_KEYS[p, d])
                        pe.wait_ge(dve_ki.sem, dve_ki[l, p, d])
                        at = ticket(pe, ("kit", l, p, d), 2, "act")
                        for i in range(NT):
                            last = tr(psum[:, at + P * i:at + P * i + P], g_ki[:, P * i:P * i + P])
                        last.then_inc(filled.sem, filled.mark(("kit", l, p, d)))
                        pe.wait_ge(act_e.sem, act_e[("kit", l, p, d)])
                        pe.wait_ge(act_e.sem, act_e[("gvt", l, p, 1)])
                        at = ticket(pe, ("gs", l, p, d), 2, "dve")
                        for i in range(NT):
                            for h in range(2):
                                hs = slice(64 * h, 64 * h + 64)
                                last = mm(psum[hs, at + P * i:at + P * i + P], g_kit[:, i, hs], g_vt[:, 5 * h + i, :],
                                          True, True)
                        last.then_inc(filled.sem, filled.mark(("gs", l, p, d)))
                        if (p, d) in GLA_LEVEL:
                            project(l, GLA_LEVEL[p, d])
                        for j in range(8 if d == 0 else 7):
                            if j < 7:
                                pe.wait_ge(dve_kq.sem, dve_kq[l, p, d, j])
                                kl, ql = g_kl[j % 2], g_ql[j % 2]
                            else:
                                kl, ql = item("gk", p), item("gq", p)
                            if j == 0:
                                ks, qs = halves(d)
                                ats = [ticket(pe, ("att", l, p, d, j, h), 1, "dve") for h in range(2)]
                                for i in range(NT):
                                    for h in range(2):
                                        hs = slice(64 * h, 64 * h + 64)
                                        last = mm(psum[ks, ats[h] + 64 * i:ats[h] + 64 * i + 64],
                                                  kl[hs, P * i:P * i + P][:, ks], ql[hs, P * i:P * i + P][:, qs],
                                                  True, True)
                                        if i == NT - 1:
                                            last.then_inc(filled.sem, filled.mark(("att", l, p, d, j, h)))
                                continue
                            ats = [ticket(pe, ("att", l, p, d, j, h), 2, "dve") for h in range(2)]
                            for i in range(NT):
                                for h in range(2):
                                    hs = slice(64 * h, 64 * h + 64)
                                    last = mm(psum[:, ats[h] + P * i:ats[h] + P * i + P], kl[hs, P * i:P * i + P],
                                              ql[hs, P * i:P * i + P], True, True)
                                    if i == NT - 1:
                                        last.then_inc(filled.sem, filled.mark(("att", l, p, d, j, h)))
                    for h in range(2):
                        hs = slice(64 * h, 64 * h + 64)
                        at = ticket(pe, ("go", l, p, h), 2, "dve")
                        pe.wait_ge(dve_e.sem, dve_e[("att", l, p, 1, 6, 1)])
                        pe.wait_ge(dve_gstates.sem, dve_gstates[l, p, 1])
                        for i in range(NT):
                            o = psum[:, at + P * i:at + P * i + P]
                            for d in range(2):
                                mm(o, g_st[d][hs, i, :], g_qi[d][hs, P * i:P * i + P], d == 0, False)
                                last = mm(o, g_vt[:, 5 * h + i, :], g_att[d][:, 5 * h + i, :], False, d == 1)
                        last.then_inc(filled.sem, filled.mark(("go", l, p, h)))
                    for h in range(2):
                        pe.wait_ge(dve_gosq.sem, dve_gosq[l, p, h])
                        sums(("goss", l, p, h), ones, [g_osqs[h]], by="act")

                def merge(key, n):
                    w = unit()
                    at = ticket(pe, (key, l, n), 2, "act")
                    for k in range(KT):
                        last = wide(at, w[:, k, :], hT[:, k, :], k == 0, k == KT - 1)
                    last.then_inc(filled.sem, filled.mark((key, l, n)))
                    unit_done()

                project(l, MLA_MERGE[0])
                for j in range(2):
                    pe.wait_ge(dve_qsq.sem, dve_qsq[l, j])
                sums(("qss", l), ones, [m_sq[0], m_sq[1]])
                pe.wait_ge(dve_kvsq.sem, dve_kvsq[l])
                sums(("kvss", l), ones, [m_sq[2]])
                pe.wait_ge(act_e.sem, act_e[(l, "misc", 0)])
                at = ticket(pe, ("krot", l), 1, "dve")
                mm(psum[64:96, at:at + TS], con[64:96, C_ROT:C_ROT + 32], item("misc")[64:96, 0:TS],
                             True, True).then_inc(filled.sem, filled.mark(("krot", l)))
                project(l, MLA_MERGE[1])
                pe.wait_ge(dve_ckv.sem, dve_ckv[l])
                for i in range(7):
                    src = (item("kvd")[:, P * i:P * i + P] if i < 4 else
                           small[:, SM["ckv"] + P * (i - 4):SM["ckv"] + P * (i - 3)] if i < 6 else
                           item("kvd")[:, TS:T])
                    at = ticket(pe, ("mv", l, i), 1, "act")
                    mm(psum[:, at:at + 512], src, small[:, SM["wv"]:SM["wv"] + 512], True, True).then_inc(filled.sem, filled.mark(("mv", l, i)))

                def head_qk(h):
                    at = ticket(pe, ("mk", l, h), 2, "act")
                    w = small[:, SM["wk"] + 64 * h:SM["wk"] + 64 * h + 64]
                    mm(psum[0:64, at:at + TS], w, item("kvd")[:, 0:TS], True, True)
                    mm(psum[0:64, at + TS:at + KEYS], w, small[:, SM["ckv"]:SM["ckv"] + PAST], True, True)
                    mm(psum[0:64, at + KEYS:at + KEYS + TP], w, item("kvd")[:, TS:T], True, True).then_inc(filled.sem, filled.mark(("mk", l, h)))
                    at = ticket(pe, ("mq", l, h), 2, "act")
                    for k in range(2):
                        w = small[:, SM["wq"] + 768 * k + 96 * h:SM["wq"] + 768 * k + 96 * h + 96]
                        last = wide(at, w, item("qd", k), k == 0, k == 1, m=slice(0, 96))
                    last.then_inc(filled.sem, filled.mark(("mq", l, h)))

                def head_rot(h):
                    pe.wait_ge(act_e.sem, act_e[("mq", l, h)])
                    at = ticket(pe, ("qrot", l, h), 1, "dve")
                    mm(psum[64:96, at:at + TS], con[64:96, C_ROT:C_ROT + 32], m_qp[h % 2][64:96, 0:TS],
                                 True, True).then_inc(filled.sem, filled.mark(("qrot", l, h)))

                def logits(h, i):
                    pe.wait_ge(act_e.sem, act_e[("mk", l, h)])
                    pe.wait_ge(dve_qr.sem, dve_qr[l, h])
                    q = slice(P * i, P * i + P)
                    k = m_k[h % 2]
                    if i < 4:
                        at = ticket(pe, ("lg", l, h, i), 2, "act")
                        mm(psum[:, at:at + TS], m_qr[h % 2][0:96, q], k[0:96, 0:TS], True, True)
                        last = mm(psum[:, at + TS:at + KEYS], m_qp[h % 2][0:96, q], k[0:96, TS:KEYS], True, True)
                    else:
                        at = ticket(pe, ("lg", l, h, i), 2, "act")
                        last = mm(psum[:, at:at + TP], m_qp[h % 2][0:96, q], k[0:96, KEYS:KEYS + TP], True, True)
                    last.then_inc(filled.sem, filled.mark(("lg", l, h, i)))

                def turn(h, i):
                    pe.wait_ge(dve_pn.sem, dve_pn[l, h, i])
                    at = ticket(pe, ("pt", l, h, i), 2, "act")
                    for j in range(6 if i < 4 else 1):
                        last = tr(psum[:, at + P * j:at + P * j + P], m_p[(5 * h + i) % 3][:, P * j:P * j + P])
                    last.then_inc(filled.sem, filled.mark(("pt", l, h, i)))

                def weigh(h, i):
                    pe.wait_ge(act_e.sem, act_e[("pt", l, h, i)])
                    hs = slice(64 * (h % 2), 64 * (h % 2) + 64)
                    at = ticket(pe, ("mlaO", l, h, i), 1, "dve")
                    ks = range(6) if i < 4 else [6]
                    for j, kt in enumerate(ks):
                        last = mm(psum[hs, at:at + P], m_v[:, kt, 64 * h:64 * h + 64],
                                  m_pt[(5 * h + i) % 2][:, P * j:P * j + P], j == 0, j == len(ks) - 1)
                    last.then_inc(filled.sem, filled.mark(("mlaO", l, h, i)))

                for key in [("mv", l, 6)]:
                    pe.wait_ge(act_e.sem, act_e[key])
                for k in range(2):
                    pe.wait_ge(dve_qn.sem, dve_qn[l, k])
                pe.wait_ge(dve_kpe.sem, dve_kpe[l])
                steps = [(h, i) for h in range(HEADS) for i in range(NT)]
                head_qk(0)
                head_rot(0)
                for n in range(len(steps) + 3):
                    if n < len(steps):
                        if steps[n][1] == 2 and steps[n][0] + 1 < HEADS:
                            head_qk(steps[n][0] + 1)
                        if steps[n][1] == 3 and steps[n][0] + 1 < HEADS:
                            head_rot(steps[n][0] + 1)
                        logits(*steps[n])
                        if steps[n][1] == MERGE_AT and steps[n][0] + 2 < len(MLA_MERGE):
                            project(l, MLA_MERGE[steps[n][0] + 2])
                    if 2 <= n < len(steps) + 2:
                        turn(*steps[n - 2])
                    if n >= 3:
                        weigh(*steps[n - 3])

                for n in range(KT):
                    def branch(key, w, o):
                        at = ticket(pe, (key, l, n), 2, "dve")
                        for k in range(4):
                            last = wide(at, w[:, k, :], acts[:, o + k, :], k == 0, k == 3)
                        last.then_inc(filled.sem, filled.mark((key, l, n)))
                    w = unit()
                    branch("ya", w[:, 0:4, :], SLOT["g", 0])
                    branch("yb", w[:, 4:8, :], SLOT["gg", 0])
                    unit_done()
                    merge("mb", n)
                    merge("mc", n)
                    pe.wait_ge(dve_e.sem, dve_e[("mlaO", l, 7, 4)])
                    w = unit()
                    branch("yc", w[:, 0:4, :], SLOT["mg", 0])
                    unit_done()
                for n in range(KT):
                    w = unit()
                    at = ticket(pe, ("wo", l, n), 2, "dve")
                    for k in range(KT):
                        if n == 0:
                            pe.wait_ge(dve_ysum.sem, dve_ysum[l, k])
                        last = wide(at, w[:, k, :], yT[:, k, :], k == 0, k == KT - 1)
                    last.then_inc(filled.sem, filled.mark(("wo", l, n)))
                    unit_done()
            mean_square(DEPTH)

        @block.scalar
        def _(act):

            def rstd(key, out, scale, eps):
                act.wait_ge(filled.sem, filled[key])
                at = place(key)
                ins = nc.scalar.activation(out, psum[:, at:at + T], ACT.Ln, bias=con[:, C_BIAS + eps:C_BIAS + eps + 1],
                                           scale=scale)
                ins.then_inc(act_e.sem, act_e.mark(key))
                act.wait_ge(act_e.sem, act_e[key])
                return nc.scalar.activation(out, out, ACT.Exp, scale=-0.5)

            def copy(key, out, src, scale=None):
                if scale is None:
                    nc.scalar.activation(out, src, ACT.Copy).then_inc(act_e.sem, act_e.mark(key))
                else:
                    nc.scalar.activation(out, src, ACT.Copy, scale=scale).then_inc(act_e.sem, act_e.mark(key))

            act.wait_ge(s_vec, 16)
            nc.scalar.activation(sc_t[:, :, :].rearrange("p a b -> p (a b)"), vec[:, VEC["c"]:VEC["c"] + 16],
                                             ACT.Sigmoid).then_inc(act_sc.sem, act_sc.mark(0))

            def project(l, it):
                act.wait_ge(filled.sem, filled[(l, *it)])
                at = place((l, *it))
                src = psum[:, at:at + T]
                if it[0] in GATES:
                    nc.scalar.activation(item(*it), src, ACT.Sigmoid).then_inc(act_sig.sem, act_sig.mark(l, it))
                elif it[0] == "wdad":
                    nc.scalar.activation(item(*it)[0:64, :], psum[0:64, at:at + T], ACT.Tanh).then_inc(act_tanh.sem, act_tanh.mark(l))
                    copy((l, *it), item(*it)[64:128, :], psum[64:128, at:at + T])
                else:
                    copy((l, *it), item(*it), src, 0.125 if it[0] == "gq" else None)

            def mod_out(l, j):
                if j >= 2:
                    act.wait_ge(filled.sem, filled[("mod", l, j - 2)])
                act.wait_ge(filled.sem, filled[("modrow", l, j)])
                at = place(("modrow", l, j))
                copy(("modrow", l, j), mod_row(j), psum[0:2, at:at + 512])

            act.wait_ge(s_con, 16)
            for j in range(MOD_GROUPS):
                mod_out(0, j)
                if j == MOD_GROUPS - 2:
                    rstd(("xss", 0), w_rs, 1.0 / D, 0).then_inc(act_xrs.sem, act_xrs.mark(0))
            for l in range(DEPTH):
                if l:
                    rstd(("xss", l), w_rs, 1.0 / D, 0).then_inc(act_xrs.sem, act_xrs.mark(l))
                for k in range(KT):
                    act.wait_ge(dve_xn.sem, dve_xn[l, k])
                    nc.scalar.activation(hT[:, k, 0:TS], hT[:, k, 0:TS], ACT.Identity, bias=mod[:, k, 0:1],
                                         scale=gs[:, k, 0:1]).then_inc(act_h.sem, act_h.mark(l, k))
                act.wait_ge(dve_zeroed.sem, dve_zeroed[l])
                for it in FIRST_ITEMS:
                    project(l, it)
                for p in range(PAIRS):
                    project(l, BESIDE[p][0])
                    act.wait_ge(dve_e.sem, dve_e[("kkss", l, p)])
                    nc.scalar.activation(w_ys, w_ys, ACT.Ln, scale=2.0 ** 20).then_inc(act_step.sem, act_step.mark())
                    act.wait_ge(act_step.sem, act_step.n)
                    nc.scalar.activation(w_ys, w_ys, ACT.Exp, scale=-0.5,
                                                     bias=con[:, C_BIAS + 2:C_BIAS + 3]).then_inc(act_rn.sem, act_rn.mark(l, p))
                    for d in range(2):
                        if d == 1:
                            act.wait_ge(dve_fac.sem, dve_fac[l, p, 0])
                        act.wait_ge(filled.sem, filled[("zw", l, p, d)])
                        at = place(("zw", l, p, d))
                        nc.scalar.activation(w_sw, psum[:, at:at + T], ACT.Sigmoid, bias=v("w0", 4 * d + p)).then_inc(act_e.sem, act_e.mark(("zw", l, p, d)))
                        act.wait_ge(filled.sem, filled[("za", l, p, d)])
                        at = place(("za", l, p, d))
                        nc.scalar.activation(w_a, psum[:, at:at + T], ACT.Sigmoid, bias=v("a0", 4 * d + p)).then_inc(act_e.sem, act_e.mark(("za", l, p, d)))
                        act.wait_ge(dve_yz.sem, dve_yz[l, p, d])
                        src, sign = ((w_ys, w_sw, w_ys), (-DECAY, -DECAY, DECAY)) if d == 0 else \
                                    ((w_sw, w_ys, w_sw), (DECAY, DECAY, -DECAY))
                        nc.scalar.activation(fac[:, 4 * d + R_, :], src[0], ACT.Exp, scale=sign[0])
                        nc.scalar.activation(fac[:, 4 * d + A_, :], src[1], ACT.Exp, scale=sign[1])
                        nc.scalar.activation(w_e, src[2], ACT.Exp, scale=sign[2])
                        nc.scalar.activation(stt[:, d, :, :], sraw[:, d, :, :], ACT.Exp, scale=-DECAY).then_inc(act_ex.sem, act_ex.mark(l, p, d))
                        for it in BESIDE[p][1:2] if d == 0 else BESIDE[p][2:4]:
                            project(l, it)
                    for steps in GROUPS:
                        def beat(r):
                            j, k = divmod(ROUNDS * p + r, KT)
                            if steps == (4,) and BESIDE_PROMPT[p] and r == 5:
                                project(l, BESIDE_PROMPT[p][0])
                            if steps == (4,) and l + 1 < DEPTH and k == KT - 1:
                                mod_out(l + 1, j)
                            if steps == (4,) and BESIDE_PROMPT[p] and r == 11:
                                project(l, BESIDE_PROMPT[p][1])

                        def bank(key, s, n=512):
                            act.wait_ge(filled.sem, filled[(key, l, p, s)])
                            at = place((key, l, p, s))
                            return psum[:, at:at + n]

                        def flat(s, name):
                            return gbuf(s % 2, name).rearrange("p a b -> p (a b)")

                        def out(s, key, name):
                            copy((key, l, p, s), flat(s, name), bank(key, s))
                        for s in steps:
                            out(s, "TB", "TB")
                            out(s, "TA", "TA")
                        for s in steps:
                            out(s, "X2", "H")
                            out(s, "X2T", "I")
                        for s in steps:
                            out(s, "X4", "X")
                            out(s, "X4T", "XT")
                        for s in steps:
                            out(s, "X8", "H")
                        beat(3)
                        for s in steps:
                            out(s, "NT", "I")
                            out(s, "N", "H")
                            J, TA = gbuf(s % 2, "J"), gbuf(s % 2, "TA")
                            copy(("AV", l, p, s), J[:, :, 64:128],
                                 bank("AV", s, 256).rearrange("p (u i) -> p u i", u=4))
                            act.wait_ge(act_e.sem, act_e[("TA", l, p, s)])
                            for d in range(2):
                                ins = nc.scalar.activation(J[:, 2 * d:2 * d + 2, 0:64],
                                                           TA[:, 2 * d, :].rearrange("p (h i) -> p h i", h=2), ACT.Copy)
                            ins.then_inc(act_J.sem, act_J.mark(l, p, s))
                        beat(5)
                        for s in steps:
                            out(s, "N2", "Off")
                            out(s, "N2T", "AakT")
                        for s in steps:
                            out(s, "N4", "H")
                        beat(7)
                        for s in steps:
                            J = gbuf(s % 2, "J").rearrange("p (w d) x -> p w (d x)", w=2)
                            src = bank("Y", s).rearrange("p (u w x) -> p w u x", u=4, w=2)
                            nc.scalar.activation(J[:, 0, :].rearrange("p (u x) -> p u x", u=4), src[:, 0, :, :],
                                                 ACT.Copy).then_inc(act_ta.sem, act_ta.mark(l, p, s))
                            copy(("Y", l, p, s), J[:, 1, :].rearrange("p (u x) -> p u x", u=4), src[:, 1, :, :])
                        for s in steps:
                            copy(("TaT", l, p, s), flat(s, "K")[:, 0:256], bank("TaT", s, 256))
                    beat(11)
                    rstd(("ovar", l, p), w_sw, 1.0 / 64, 1).then_inc(act_ors.sem, act_ors.mark(l, p))

                for it in END_ITEMS + REST_ITEMS:
                    project(l, it)

                for p in range(2):
                    for h in range(2):
                        act.wait_ge(filled.sem, filled[("gvt", l, p, h)])
                        at = place(("gvt", l, p, h))
                        copy(("gvt", l, p, h), g_vt[:, 5 * h:5 * h + 5, :].rearrange("p a b -> p (a b)"),
                             psum[:, at:at + T])
                    for d in range(2):
                        act.wait_ge(dve_gax.sem, dve_gax[l, p, d])
                        nc.scalar.activation(g_ax, g_ax, ACT.Exp, scale=-1.0).then_inc(act_step.sem, act_step.mark())
                        act.wait_ge(act_step.sem, act_step.n)
                        nc.scalar.activation(g_ax, g_ax, ACT.Ln, bias=con[:, C_BIAS + 3:C_BIAS + 4]).then_inc(act_gln.sem, act_gln.mark(l, p, d))
                        act.wait_ge(dve_gz.sem, dve_gz[l, p, d])
                        z = g_b if d == 0 else g_z
                        nc.scalar.activation(g_eq, z if d == 0 else g_d, ACT.Exp, scale=1.0 / 16)
                        nc.scalar.activation(g_ek, g_d if d == 0 else z, ACT.Exp, scale=1.0 / 16)
                        nc.scalar.activation(g_dec[:, :], g_b[:, P - 1::P], ACT.Exp, scale=1.0 / 16).then_inc(act_gexp.sem, act_gexp.mark(l, p, d))
                        project(l, GLA_KEYS[p, d])
                        act.wait_ge(filled.sem, filled[("kit", l, p, d)])
                        at = place(("kit", l, p, d))
                        copy(("kit", l, p, d), g_kit[:, :, :].rearrange("p a b -> p (a b)"), psum[:, at:at + T])
                        for j in range(7):
                            if j == 3 and (p, d) in GLA_LEVEL:
                                project(l, GLA_LEVEL[p, d])
                            act.wait_ge(dve_lvl.sem, dve_lvl[l, p, d, j])
                            nc.scalar.activation(g_e[j % 2], g_e[j % 2], ACT.Exp, scale=1.0 / 16).then_inc(act_le.sem, act_le.mark(l, p, d, j))
                    for h in range(2):
                        rstd(("goss", l, p, h), g_rs[h], 1.0 / P, 0).then_inc(act_grs.sem, act_grs.mark(l, p, h))

                act.wait_ge(dve_gla_out.sem, dve_gla_out[l, 3])
                project(l, MLA_MERGE[0])
                rstd(("qss", l), m_r[0], 1.0 / 256, 0).then_inc(act_qrs.sem, act_qrs.mark(l))
                rstd(("kvss", l), m_r[1], 1.0 / 128, 0).then_inc(act_kvrs.sem, act_kvrs.mark(l))
                project(l, MLA_MERGE[1])
                for i in range(7):
                    act.wait_ge(filled.sem, filled[("mv", l, i)])
                    at = place(("mv", l, i))
                    copy(("mv", l, i), m_v[:, i, :], psum[:, at:at + 512])

                def head_qk(h):
                    act.wait_ge(filled.sem, filled[("mk", l, h)])
                    at = place(("mk", l, h))
                    copy(("mk", l, h), m_k[h % 2][0:64, :], psum[0:64, at:at + KEYS + TP])
                    act.wait_ge(filled.sem, filled[("mq", l, h)])
                    at = place(("mq", l, h))
                    nc.scalar.activation(m_qr[h % 2][0:64, :], psum[0:64, at:at + TS], ACT.Copy, scale=SCALE)
                    copy(("mq", l, h), m_qp[h % 2][0:96, :], psum[0:96, at:at + T], SCALE)

                steps = [(h, i) for h in range(HEADS) for i in range(NT)]
                head_qk(0)
                for n in range(len(steps) + 2):
                    if n < len(steps):
                        h, i = steps[n]
                        if i == 2 and h + 1 < HEADS:
                            head_qk(h + 1)
                        w = KEYS if i < 4 else TP
                        act.wait_ge(filled.sem, filled[("lg", l, h, i)])
                        at = place(("lg", l, h, i))
                        act.wait_ge(dve_nm.sem, dve_nm[l, h, i])
                        nc.scalar.activation(m_p[n % 3][:, 0:w], psum[:, at:at + w], ACT.Exp,
                                                      bias=m_nm[:, n:n + 1], accum_out=m_sum[:, n:n + 1]).then_inc(act_e.sem, act_e.mark(("lg", l, h, i)))
                        if i == MERGE_AT and h + 2 < len(MLA_MERGE):
                            project(l, MLA_MERGE[h + 2])
                    if n >= 2:
                        h, i = steps[n - 2]
                        w = KEYS if i < 4 else TP
                        act.wait_ge(filled.sem, filled[("pt", l, h, i)])
                        at = place(("pt", l, h, i))
                        copy(("pt", l, h, i), m_pt[n % 2][:, 0:w], psum[:, at:at + w])
                for n in range(KT):
                    act.wait_ge(act_e.sem, act_e[(l, "ma", n)])
                    nc.scalar.activation(acts[:, SLOT_MERGE + n, :], acts[:, SLOT_MERGE + n, :],
                                         ACT.Sigmoid).then_inc(act_ma.sem, act_ma.mark(l, n))
                    for j, (key, y) in ((1, ("mb", "yb")), (2, ("mc", "yc"))):
                        if n:
                            act.wait_ge(dve_e.sem, dve_e[(y, l, n - 1)])
                        act.wait_ge(filled.sem, filled[(key, l, n)])
                        at = place((key, l, n))
                        nc.scalar.activation(f_s[j], psum[:, at:at + T], ACT.Sigmoid).then_inc(act_e.sem, act_e.mark((key, l, n)))
            rstd(("xss", DEPTH), w_rs, 1.0 / D, 0).then_inc(act_xrs.sem, act_xrs.mark(DEPTH))

        @block.vector
        def _(dve):
            V = nc.vector


            def ttn(out, a, b, op):
                return V.tensor_tensor(out, a, b, op)

            def mul(out, a, b):
                return V.tensor_tensor(out, a, b, ALU.mult)

            def ts(out, a, s1, s2=None, op0=ALU.mult, op1=None):
                if s2 is None:
                    return V.tensor_scalar(out, a, s1, None, op0)
                return V.tensor_scalar(out, a, s1, s2, op0, op1)

            def stt3(out, a, s, b, op0, op1):
                return V.scalar_tensor_tensor(out=out, in0=a, scalar=s, in1=b, op0=op0, op1=op1)

            def mod_columns(l, j):
                dve.wait_ge(filled.sem, filled[("mod", l, j)])
                at = place(("mod", l, j))
                V.tensor_copy(mod_new[:, 4 * j:4 * j + 4, :],
                              psum[:, at:at + 8].rearrange("p (a b) -> p a b", a=4)).then_inc(dve_e.sem, dve_e.mark(("mod", l, j)))

            dve.wait_ge(s_vec, 16)
            dve.wait_ge(act_sc.sem, act_sc[0])
            mul(sc[:, :, :].rearrange("p a b -> p (a b)"), sc_t[:, :, :].rearrange("p a b -> p (a b)"),
                            vec[:, VEC["c"]:VEC["c"] + 16]).then_inc(dve_sc.sem, dve_sc.mark(0))
            dve.wait_ge(s_x, 16)
            for k in range(KT):
                mul(acts[:, k, :], hT[:, k, :], hT[:, k, :]).then_inc(dve_xsq.sem, dve_xsq.mark(0, k))
            for j in range(MOD_GROUPS):
                mod_columns(0, j)
            for l in range(DEPTH):
                dve.wait_ge(s_vec, 16 * (l + 1))
                ts(omka[:, :], vec[:, VEC["k_a"]:VEC["k_a"] + 4], -1.0, 1.0, ALU.mult, ALU.add).then_inc(dve_step.sem, dve_step.mark())
                dve.wait_ge(dve_e.sem, dve_e[("mod", l, MOD_GROUPS - 1)])
                ttn(mod[:, :, :], mod_new[:, :, :],
                    vec[:, VEC["b_mod"]:VEC["b_mod"] + 24].unsqueeze(2).broadcast_to([P, 24, 2]), ALU.add).then_inc(dve_step.sem, dve_step.mark())
                dve.wait_ge(dve_step.sem, dve_step.n)
                stt3(gs[:, :, :], mod[:, 8:16, :], 1.0,
                           vec[:, VEC["norm_g"]:VEC["norm_g"] + 8].unsqueeze(2).broadcast_to([P, 8, 2]),
                           ALU.add, ALU.mult).then_inc(dve_step.sem, dve_step.mark())
                dve.wait_ge(dve_step.sem, dve_step.n)
                dve.wait_ge(act_xrs.sem, act_xrs[l])
                if l:
                    dve.wait_ge(s_keep, 16 * KT)
                for k in range(KT + 1):
                    if k < KT:
                        mul(hT[:, k, :], hT[:, k, :], w_rs).then_inc(dve_xn.sem, dve_xn.mark(l, k))
                    if k:
                        dve.wait_ge(dve_xn.sem, dve_xn[l, k - 1])
                        ts(hT[:, k - 1, TS:T], hT[:, k - 1, TS:T], gs[:, k - 1, 1:2], mod[:, k - 1, 1:2],
                           ALU.mult, ALU.add).then_inc(dve_h.sem, dve_h.mark(l, k - 1))
                for g in range(2):
                    for name in ("XT", "X", "Off", "AakT", "ArbT", "ArkT"):
                        ins = V.memset(gbuf(g, name), 0.0)
                ins.then_inc(dve_zeroed.sem, dve_zeroed.mark(l))
                dve.wait_ge(dve_zeroed.sem, dve_zeroed[l])

                def gates(items):
                    for it in items:
                        if it[0] in GATES:
                            dve.wait_ge(filled.sem, filled[(l, *it)])
                            at = place((l, *it))
                            dve.wait_ge(act_sig.sem, act_sig[l, it])
                            mul(item(*it), item(*it), psum[:, at:at + T]).then_inc(dve_e.sem, dve_e.mark((l, *it)))

                if l == 0:
                    dve.wait_ge(pool_gate.sem, pool_gate[0])
                    dve.wait_ge(s_small, 16)
                for p in range(PAIRS):
                    k_, r_, v_ = item("k", p), item("r", p), item("v", p)
                    dve.wait_ge(act_e.sem, act_e[(l, "v", p)])
                    ts(w_kk, k_, v("k_k", p)).then_inc(dve_step.sem, dve_step.mark())
                    dve.wait_ge(dve_step.sem, dve_step.n)
                    mul(w_ys, w_kk, w_kk).then_inc(dve_kksq.sem, dve_kksq.mark(l, p))
                    dve.wait_ge(filled.sem, filled[("kkss", l, p)])
                    at = place(("kkss", l, p))
                    ts(w_ys, psum[:, at:at + T], 1e-24, op0=ALU.max).then_inc(dve_e.sem, dve_e.mark(("kkss", l, p)))
                    dve.wait_ge(act_rn.sem, act_rn[l, p])
                    mul(w_kk, w_kk, w_ys).then_inc(dve_step.sem, dve_step.mark())
                    dve.wait_ge(dve_step.sem, dve_step.n)
                    for d in range(2):
                        dve.wait_ge(act_e.sem, act_e[("zw", l, p, d)])
                        if d == 0 and p:
                            dve.wait_ge(dve_state_done.sem, dve_state_done[l, p - 1])
                        V.tensor_tensor_scan(w_ys, gate[:, :], w_sw, 0.0, ALU.mult, ALU.add).then_inc(dve_step.sem, dve_step.mark())
                        dve.wait_ge(dve_step.sem, dve_step.n)
                        ys3 = w_ys.rearrange("p (n t) -> p n t", n=NT)
                        ins = V.tensor_copy(sraw[:, d, 0, :], w_ys[:, 63::P])
                        ins.then_inc(dve_step.sem, dve_step.mark())
                        dve.wait_ge(dve_step.sem, dve_step.n)
                        ttn(sraw[:, d, 1, :], w_ys[:, P - 1::P], sraw[:, d, 0, :], ALU.subtract).then_inc(dve_step.sem, dve_step.mark())
                        dve.wait_ge(dve_step.sem, dve_step.n)
                        ttn(ys3, ys3, sraw[:, d, 0, :].unsqueeze(2).broadcast_to([P, NT, P]), ALU.subtract).then_inc(dve_step.sem, dve_step.mark())
                        dve.wait_ge(dve_step.sem, dve_step.n)
                        ttn(w_sw, w_ys, w_sw, ALU.subtract).then_inc(dve_yz.sem, dve_yz.mark(l, p, d))
                        dve.wait_ge(act_e.sem, act_e[("za", l, p, d)])
                        mul(fac[:, 4 * d + B_, :], w_kk, w_a)
                        ts(fac[:, 4 * d + K_, :], w_a, v("k_a", p), omka[:, p:p + 1], ALU.mult, ALU.add).then_inc(dve_step.sem, dve_step.mark())
                        dve.wait_ge(dve_step.sem, dve_step.n)
                        mul(fac[:, 4 * d + K_, :], fac[:, 4 * d + K_, :], k_).then_inc(dve_step.sem, dve_step.mark())
                        dve.wait_ge(dve_step.sem, dve_step.n)
                        dve.wait_ge(act_ex.sem, act_ex[l, p, d])
                        mul(fac[:, 4 * d + R_, :], fac[:, 4 * d + R_, :], r_)
                        stt3(fac[:, 4 * d + A_, :], fac[:, 4 * d + A_, :], -1.0, w_kk, ALU.mult, ALU.mult)
                        mul(fac[:, 4 * d + B_, :], fac[:, 4 * d + B_, :], w_e)
                        mul(fac[:, 4 * d + K_, :], fac[:, 4 * d + K_, :], w_e).then_inc(dve_fac.sem, dve_fac.mark(l, p, d))
                    mul(trn[:, 0, 0:3], stt[:, 0, 1, 0:3], stt[:, 0, 0, 1:4])
                    ins = mul(trn[:, 1, 1:4], stt[:, 1, 0, 1:4], stt[:, 1, 1, 0:3])
                    for d in range(2):
                        s0 = small[:, SM["s_rw"] + P * (4 * d + p):SM["s_rw"] + P * (4 * d + p) + P]
                        i0 = 0 if d == 0 else 3
                        ins = ts(st[:, d, :], s0, stt[:, d, d, i0:i0 + 1])
                    ins.then_inc(dve_state.sem, dve_state.mark(l, p, 0))
                    dve.wait_ge(dve_state.sem, dve_state[l, p, 0])
                    dve.wait_ge(dve_fac.sem, dve_fac[l, p, 1])
                    ts(r_, r_, v("r_k", p)).then_inc(dve_step.sem, dve_step.mark())
                    dve.wait_ge(dve_step.sem, dve_step.n)
                    mul(r_, r_, k_).then_inc(dve_rkr.sem, dve_rkr.mark(l, p))
                    dve.wait_ge(dve_rkr.sem, dve_rkr[l, p])
                    V.memset(k_, 0.0).then_inc(dve_step.sem, dve_step.mark())
                    dve.wait_ge(dve_step.sem, dve_step.n)
                    gates(BESIDE[p])

                    for steps in GROUPS:
                        def tile(d, s):
                            return s if s == 4 or d == 0 else 3 - s

                        def bank(key, s, n=512):
                            dve.wait_ge(filled.sem, filled[(key, l, p, s)])
                            at = place((key, l, p, s))
                            return psum[:, at:at + n]

                        def beat(r):
                            j, k = divmod(ROUNDS * p + r, KT)
                            if steps == (4,) and l + 1 < DEPTH and k == 2 and j:
                                mod_columns(l + 1, j - 1)

                        def masked(s, key, w, name, m, last=True):
                            src = bank(key, s, 1024).rearrange("p (h d w x) -> p w d h x", h=2, d=2, w=2)[:, w]
                            ins = V.copy_predicated(gbuf(s % 2, name).rearrange("p (d h) x -> p d h x", d=2),
                                                    masks[:, m, :, :].unsqueeze(2).broadcast_to([P, 2, 2, P]), src)
                            if last:
                                ins.then_inc(dve_e.sem, dve_e.mark((key, l, p, s)))

                        def add(s, key, name):
                            B = gbuf(s % 2, name).rearrange("p a b -> p (a b)")
                            ttn(B, bank(key, s), B, ALU.add).then_inc(dve_e.sem, dve_e.mark((key, l, p, s)))
                        for s in steps:
                            masked(s, "Ab", 0, "XT", M_XT, last=False)
                            masked(s, "Ab", 1, "ArbT", M_INC)
                            masked(s, "Ak", 0, "AakT", M_STR, last=False)
                            masked(s, "Ak", 1, "ArkT", M_INC)
                            masked(s, "Aab", 0, "X", M_X, last=False)
                            masked(s, "Aab", 0, "Off", M_OFF)
                            dve.wait_ge(dve_e.sem, dve_e[("Ab", l, p, s)])
                            ttn(gbuf(s % 2, "G"), gbuf(s % 2, "XT"),
                                            ident.unsqueeze(1).broadcast_to([P, 4, P]), ALU.add).then_inc(dve_FT.sem, dve_FT.mark(l, p, s))
                        for s in steps:
                            dve.wait_ge(dve_FT.sem, dve_FT[l, p, s])
                            add(s, "GT", "G")
                        beat(2)
                        for s in steps:
                            dve.wait_ge(dve_e.sem, dve_e[("GT", l, p, s)])
                            add(s, "HT", "G")
                        for s in steps:
                            dve.wait_ge(dve_e.sem, dve_e[("HT", l, p, s)])
                            add(s, "T16T", "G")
                        for s in steps:
                            V.tensor_copy(gbuf(s % 2, "K").rearrange("p a b -> p (a b)"), bank("Y1", s)).then_inc(dve_e.sem, dve_e.mark(("Y1", l, p, s)))
                            dve.wait_ge(act_e.sem, act_e[("NT", l, p, s)])
                            ttn(gbuf(s % 2, "I"), gbuf(s % 2, "I"),
                                            ident.unsqueeze(1).broadcast_to([P, 4, P]), ALU.add).then_inc(dve_MT1.sem, dve_MT1.mark(l, p, s))
                        beat(6)
                        for s in steps:
                            dve.wait_ge(dve_MT1.sem, dve_MT1[l, p, s])
                            add(s, "MT2", "I")
                        for s in steps:
                            dve.wait_ge(dve_e.sem, dve_e[("MT2", l, p, s)])
                            add(s, "MT3", "I")
                        beat(10)
                        for s in steps:
                            J, K = gbuf(s % 2, "J"), gbuf(s % 2, "K")
                            src = bank("U", s, 256).rearrange("p (d x) -> p d x", d=2)
                            dve.wait_ge(act_e.sem, act_e[("Y", l, p, s)])
                            ttn(K[:, 2:4, :], src, J[:, 2:4, :], ALU.add).then_inc(dve_e.sem, dve_e.mark(("U", l, p, s)))
                            if s != 3:
                                src = bank("S", s, 256)
                                if s == 0 and l * 4 + p:
                                    dve.wait_ge(s_sto, 16 * (l * 4 + p))
                                for d in range(2):
                                    i = tile(d, s)
                                    g = (trn[:, d, i:i + 1] if s < 3 else stt[:, d, 1 - d, 4:5])
                                    ins = stt3(st_t[:, d, :], src[:, P * d:P * d + P], g, bd, ALU.mult, ALU.mult)
                                ins.then_inc(dve_e.sem, dve_e.mark(("S", l, p, s)))
                                if s == 4:
                                    V.memset(trn[:, :, :], 0.0).then_inc(dve_new_state.sem, dve_new_state.mark(l, p))
                            if s < 3:
                                dve.wait_ge(dve_e.sem, dve_e[("S", l, p, s)])
                                for d in range(2):
                                    i = tile(d, s)
                                    ins = stt3(st[:, d, :], st[:, d, :], trn[:, d, i:i + 1], st_t[:, d, :],
                                               ALU.mult, ALU.add)
                                ins.then_inc(dve_state.sem, dve_state.mark(l, p, s + 1))
                                dve.wait_ge(dve_state.sem, dve_state[l, p, s + 1])
                            elif s == 3:
                                dve.wait_ge(filled.sem, filled[("O", l, p, 3)])
                                V.memset(st[:, :, :], 0.0).then_inc(dve_state.sem, dve_state.mark(l, p, 4))
                            src = bank("O", s, 256)
                            for d in range(2):
                                o = k_[:, P * tile(d, s):P * tile(d, s) + P]
                                ins = ttn(o, o, src[:, P * d:P * d + P], ALU.add)
                                if s == 4 and d == 0:
                                    ins.then_inc(dve_step.sem, dve_step.mark())
                                    dve.wait_ge(dve_step.sem, dve_step.n)
                            ins.then_inc(dve_e.sem, dve_e.mark(("O", l, p, s)))
                    dve.wait_ge(filled.sem, filled[("bonus", l, p)])
                    at = place(("bonus", l, p))
                    mul(w_a, psum[:, at:at + T], v_).then_inc(dve_e.sem, dve_e.mark(("bonus", l, p)))
                    dve.wait_ge(dve_e.sem, dve_e[("O", l, p, 4)])
                    dve.wait_ge(filled.sem, filled[("omean", l, p)])
                    at = place(("omean", l, p))
                    stt3(w_kk, psum[:, at:at + T], -1.0 / 64, k_, ALU.mult, ALU.add).then_inc(dve_e.sem, dve_e.mark(("omean", l, p)))
                    dve.wait_ge(dve_e.sem, dve_e[("omean", l, p)])
                    mul(w_ys, w_kk, w_kk).then_inc(dve_osq.sem, dve_osq.mark(l, p))
                    dve.wait_ge(act_ors.sem, act_ors[l, p])
                    mul(w_kk, w_kk, w_sw).then_inc(dve_step.sem, dve_step.mark())
                    dve.wait_ge(dve_step.sem, dve_step.n)
                    ts(w_kk, w_kk, v("ln_g", p), v("ln_b", p), ALU.mult, ALU.add).then_inc(dve_step.sem, dve_step.mark())
                    dve.wait_ge(dve_step.sem, dve_step.n)
                    dve.wait_ge(dve_e.sem, dve_e[("bonus", l, p)])
                    ttn(w_kk, w_kk, w_a, ALU.add).then_inc(dve_step.sem, dve_step.mark())
                    dve.wait_ge(dve_step.sem, dve_step.n)
                    mul(item("g", p), item("g", p), w_kk).then_inc(dve_state_done.sem, dve_state_done.mark(l, p))
                    dve.wait_ge(dve_state_done.sem, dve_state_done[l, p])
                if l + 1 < DEPTH:
                    mod_columns(l + 1, MOD_GROUPS - 1)
                dve.wait_ge(s_sto, 16 * (l * 4 + 4))
                for d in range(2):
                    ins = V.memset(g_att[d], 0.0)
                ins.then_inc(dve_rwkv_done.sem, dve_rwkv_done.mark(l))
                dve.wait_ge(dve_rwkv_done.sem, dve_rwkv_done[l])
                gates(REST_ITEMS)

                for p in range(2):
                    q_, k_ = item("gq", p), item("gk", p)
                    for d in range(2):
                        dve.wait_ge(filled.sem, filled[("gx", l, p, d)])
                        at = place(("gx", l, p, d))
                        ts(g_x, psum[:, at:at + T], v("ab", 2 * d + p), op0=ALU.add).then_inc(dve_e.sem, dve_e.mark(("gx", l, p, d)))
                        dve.wait_ge(dve_e.sem, dve_e[("gx", l, p, d)])
                        stt3(g_ax, g_x, -1.0, g_x, ALU.mult, ALU.max).then_inc(dve_gax.sem, dve_gax.mark(l, p, d))
                        dve.wait_ge(act_gln.sem, act_gln[l, p, d])
                        stt3(g_z, g_x, 0.0, g_ax, ALU.min, ALU.subtract).then_inc(dve_step.sem, dve_step.mark())
                        dve.wait_ge(dve_step.sem, dve_step.n)
                        V.tensor_tensor_scan(g_b, gate[:, :], g_z, 0.0, ALU.mult, ALU.add).then_inc(dve_step.sem, dve_step.mark())
                        dve.wait_ge(dve_step.sem, dve_step.n)
                        z = g_b
                        if d == 1:
                            ttn(g_z, g_b, g_z, ALU.subtract).then_inc(dve_step.sem, dve_step.mark())
                            dve.wait_ge(dve_step.sem, dve_step.n)
                            z = g_z
                        z3 = z.rearrange("p (n t) -> p n t", n=NT)
                        b3 = g_b.rearrange("p (n t) -> p n t", n=NT)
                        ttn(g_d.rearrange("p (n t) -> p n t", n=NT),
                                        b3[:, :, P - 1:P].broadcast_to([P, NT, P]), z3, ALU.subtract).then_inc(dve_gz.sem, dve_gz.mark(l, p, d))
                        dve.wait_ge(act_gexp.sem, act_gexp[l, p, d])
                        dve.wait_ge(act_e.sem, act_e[(l, "gk", p)])
                        mul(g_qi[d], g_eq, q_)
                        mul(g_ki, g_ek, k_).then_inc(dve_ki.sem, dve_ki.mark(l, p, d))
                        def level(j):
                            h = LEVELS[j]
                            zz = z.rearrange("p (n c) -> p n c", c=2 * h)
                            ee = g_e[j % 2].rearrange("p (n c) -> p n c", c=2 * h)
                            ref = g_b.rearrange("p (n c) -> p n c", c=2 * h)[:, :, h - 1:h]
                            ref = ref.broadcast_to([P, T // (2 * h), h])
                            ttn(ee[:, :, 0:h], ref, zz[:, :, 0:h], ALU.subtract)
                            ttn(ee[:, :, h:2 * h], zz[:, :, h:2 * h], ref, ALU.subtract).then_inc(dve_lvl.sem, dve_lvl.mark(l, p, d, j))
                        dve.wait_ge(dve_ki.sem, dve_ki[l, p, d])
                        level(0)
                        level(1)
                        gates([GLA_KEYS[p, d]])
                        dve.wait_ge(filled.sem, filled[("gs", l, p, d)])
                        at = place(("gs", l, p, d))
                        o = SM["s_gla"] + P * (2 * d + p)
                        order = (0, 1, 2, 3) if d == 0 else (3, 2, 1, 0)
                        V.memset(g_st[d][:, 4, :], 0.0)
                        V.tensor_copy(g_st[d][:, order[0], :], small[:, o:o + P]).then_inc(dve_step.sem, dve_step.mark())
                        dve.wait_ge(dve_step.sem, dve_step.n)
                        for i, j in zip(order, order[1:]):
                            stt3(g_st[d][:, j, :], g_st[d][:, i, :], g_dec[:, i:i + 1],
                                       psum[:, at + P * i:at + P * i + P], ALU.mult, ALU.add).then_inc(dve_step.sem, dve_step.mark())
                            dve.wait_ge(dve_step.sem, dve_step.n)
                        V.tensor_copy(g_new[:, 2 * p + d, :], psum[:, at + 4 * P:at + 5 * P]).then_inc(dve_e.sem, dve_e.mark(("gs", l, p, d)))
                        V.memset(g_x[:, 0:1], 0.0).then_inc(dve_gstates.sem, dve_gstates.mark(l, p, d))

                        def attention(j):
                            m = M_LEVEL + j if j < 7 else M_ID
                            mask = masks[:, m, d, :].unsqueeze(1).broadcast_to([P, NT, P])
                            for h in range(2):
                                dve.wait_ge(filled.sem, filled[("att", l, p, d, j, h)])
                                at = place(("att", l, p, d, j, h))
                                if j:
                                    dve.wait_ge(dve_e.sem, dve_e[("att", l, p, d, j - 1, h)])
                                elif d:
                                    dve.wait_ge(dve_e.sem, dve_e[("att", l, p, 0, 7, h)])
                                if j == 0:
                                    ks, qs = halves(d)
                                    V.tensor_copy(g_att[d][ks, 5 * h:5 * h + 5, qs],
                                                  psum[ks, at:at + 64 * NT].rearrange("p (n t) -> p n t", n=NT)).then_inc(dve_e.sem, dve_e.mark(("att", l, p, d, j, h)))
                                    continue
                                if j == 7:
                                    V.copy_predicated(g_att[1][:, 5 * h:5 * h + 5, :], mask,
                                                      psum[:, at:at + T].rearrange("p (n t) -> p n t", n=NT))
                                ins = V.copy_predicated(g_att[d][:, 5 * h:5 * h + 5, :], mask,
                                                        psum[:, at:at + T].rearrange("p (n t) -> p n t", n=NT))
                                ins.then_inc(dve_e.sem, dve_e.mark(("att", l, p, d, j, h)))
                        for j in range(8):
                            if j < 7:
                                dve.wait_ge(act_le.sem, act_le[l, p, d, j])
                                mul(g_kl[j % 2], g_e[j % 2], k_)
                                mul(g_ql[j % 2], g_e[j % 2], q_).then_inc(dve_kq.sem, dve_kq.mark(l, p, d, j))
                                dve.wait_ge(dve_kq.sem, dve_kq[l, p, d, j])
                            if j + 2 < 7:
                                level(j + 2)
                            if j == 2 and (p, d) in GLA_LEVEL:
                                gates([GLA_LEVEL[p, d]])
                            if j:
                                attention(j - 1)
                        if d == 0:
                            attention(7)
                    for h in range(2):
                        dve.wait_ge(filled.sem, filled[("go", l, p, h)])
                        at = place(("go", l, p, h))
                        V.tensor_copy(g_os[h], psum[:, at:at + T]).then_inc(dve_e.sem, dve_e.mark(("go", l, p, h)))
                        dve.wait_ge(dve_e.sem, dve_e[("go", l, p, h)])
                        mul(g_osqs[h], g_os[h], g_os[h]).then_inc(dve_gosq.sem, dve_gosq.mark(l, p, h))
                    for h in range(2):
                        dve.wait_ge(act_grs.sem, act_grs[l, p, h])
                        mul(g_os[h], g_os[h], g_rs[h]).then_inc(dve_step.sem, dve_step.mark())
                        dve.wait_ge(dve_step.sem, dve_step.n)
                        g_ = item("gg", 2 * p + h)
                        stt3(g_, g_os[h], v("gla_g"), g_, ALU.mult, ALU.mult).then_inc(dve_gla_out.sem, dve_gla_out.mark(l, 2 * p + h))
                        dve.wait_ge(dve_gla_out.sem, dve_gla_out[l, 2 * p + h])
                dve.wait_ge(pool_gla_stored.sem, pool_gla_stored[l])

                for k in range(2):
                    mul(m_sq[k], item("qd", k), item("qd", k)).then_inc(dve_qsq.sem, dve_qsq.mark(l, k))
                dve.wait_ge(act_e.sem, act_e[(l, "kvd", 0)])
                mul(m_sq[2], item("kvd"), item("kvd")).then_inc(dve_kvsq.sem, dve_kvsq.mark(l))
                dve.wait_ge(act_qrs.sem, act_qrs[l])
                for k in range(2):
                    stt3(item("qd", k), item("qd", k), v("qn_g", k), m_r[0], ALU.mult, ALU.mult).then_inc(dve_qn.sem, dve_qn.mark(l, k))
                dve.wait_ge(act_kvrs.sem, act_kvrs[l])
                stt3(item("kvd"), item("kvd"), v("kvn_g"), m_r[1], ALU.mult, ALU.mult).then_inc(dve_ckv.sem, dve_ckv.mark(l))
                rr = slice(64, 96)
                dve.wait_ge(filled.sem, filled[("krot", l)])
                at = place(("krot", l))
                mul(m_t[rr, 0:TS], psum[rr, at:at + TS], con[rr, C_SIN:C_SIN + TS]).then_inc(dve_e.sem, dve_e.mark(("krot", l)))
                mul(m_k[0][rr, 0:TS], item("misc")[rr, 0:TS], con[rr, C_COS:C_COS + TS])
                for b in range(2):
                    V.tensor_copy(m_k[b][rr, TS:KEYS], small[rr, SM["kpe"]:SM["kpe"] + PAST])
                    ins = V.tensor_copy(m_k[b][rr, KEYS:KEYS + TP], item("misc")[rr, TS:T])
                ins.then_inc(dve_step.sem, dve_step.mark())
                dve.wait_ge(dve_step.sem, dve_step.n)
                dve.wait_ge(dve_e.sem, dve_e[("krot", l)])
                ttn(m_k[0][rr, 0:TS], m_k[0][rr, 0:TS], m_t[rr, 0:TS], ALU.add).then_inc(dve_step.sem, dve_step.mark())
                dve.wait_ge(dve_step.sem, dve_step.n)
                V.tensor_copy(m_k[1][rr, 0:TS], m_k[0][rr, 0:TS]).then_inc(dve_kpe.sem, dve_kpe.mark(l))

                def head_rot(h):
                    dve.wait_ge(act_e.sem, act_e[("mq", l, h)])
                    dve.wait_ge(filled.sem, filled[("qrot", l, h)])
                    at = place(("qrot", l, h))
                    mul(m_t[rr, 0:TS], psum[rr, at:at + TS], con[rr, C_SIN:C_SIN + TS]).then_inc(dve_e.sem, dve_e.mark(("qrot", l, h)))
                    mul(m_qr[h % 2][rr, :], m_qp[h % 2][rr, 0:TS], con[rr, C_COS:C_COS + TS]).then_inc(dve_step.sem, dve_step.mark())
                    dve.wait_ge(dve_step.sem, dve_step.n)
                    dve.wait_ge(dve_e.sem, dve_e[("qrot", l, h)])
                    ttn(m_qr[h % 2][rr, :], m_qr[h % 2][rr, :], m_t[rr, 0:TS], ALU.add).then_inc(dve_qr.sem, dve_qr.mark(l, h))
                    dve.wait_ge(dve_qr.sem, dve_qr[l, h])

                steps = [(h, i) for h in range(HEADS) for i in range(NT)]
                head_rot(0)
                for n in range(len(steps) + 3):
                    if n < len(steps):
                        h, i = steps[n]
                        if i == 3 and h + 1 < HEADS:
                            head_rot(h + 1)
                        w = KEYS if i < 4 else TP
                        dve.wait_ge(filled.sem, filled[("lg", l, h, i)])
                        at = place(("lg", l, h, i))
                        V.reduce_max(m_nm[:, n:n + 1], psum[:, at:at + w], AX.X, negate=True).then_inc(dve_nm.sem, dve_nm.mark(l, h, i))
                    if 1 <= n <= len(steps):
                        h, i = steps[n - 1]
                        w = KEYS if i < 4 else TP
                        dve.wait_ge(act_e.sem, act_e[("lg", l, h, i)])
                        V.reciprocal(m_rec[:, n - 1:n], m_sum[:, n - 1:n]).then_inc(dve_step.sem, dve_step.mark())
                        dve.wait_ge(dve_step.sem, dve_step.n)
                        ts(m_p[(n - 1) % 3][:, 0:w], m_p[(n - 1) % 3][:, 0:w], m_rec[:, n - 1:n]).then_inc(dve_pn.sem, dve_pn.mark(l, h, i))
                    if n >= 3:
                        h, i = steps[n - 3]
                        hs = slice(64 * (h % 2), 64 * (h % 2) + 64)
                        dve.wait_ge(filled.sem, filled[("mlaO", l, h, i)])
                        at = place(("mlaO", l, h, i))
                        o = item("mg", h // 2)[hs, P * i:P * i + P]
                        mul(o, o, psum[hs, at:at + P]).then_inc(dve_e.sem, dve_e.mark(("mlaO", l, h, i)))

                for n in range(KT):
                    dve.wait_ge(act_ma.sem, act_ma[l, n])
                    dve.wait_ge(filled.sem, filled[("ya", l, n)])
                    at = place(("ya", l, n))
                    mul(yT[:, n, :], acts[:, SLOT_MERGE + n, :], psum[:, at:at + T]).then_inc(dve_e.sem, dve_e.mark(("ya", l, n)))
                    dve.wait_ge(act_e.sem, act_e[("mb", l, n)])
                    dve.wait_ge(filled.sem, filled[("yb", l, n)])
                    at = place(("yb", l, n))
                    mul(f_t[0], f_s[1], psum[:, at:at + T]).then_inc(dve_e.sem, dve_e.mark(("yb", l, n)))
                    dve.wait_ge(dve_e.sem, dve_e[("yb", l, n)])
                    ttn(yT[:, n, :], yT[:, n, :], f_t[0], ALU.add).then_inc(dve_step.sem, dve_step.mark())
                    dve.wait_ge(dve_step.sem, dve_step.n)
                    dve.wait_ge(act_e.sem, act_e[("mc", l, n)])
                    dve.wait_ge(filled.sem, filled[("yc", l, n)])
                    at = place(("yc", l, n))
                    mul(f_t[1], f_s[2], psum[:, at:at + T]).then_inc(dve_e.sem, dve_e.mark(("yc", l, n)))
                    dve.wait_ge(dve_e.sem, dve_e[("yc", l, n)])
                    ttn(yT[:, n, :], yT[:, n, :], f_t[1], ALU.add).then_inc(dve_ysum.sem, dve_ysum.mark(l, n))
                    dve.wait_ge(dve_ysum.sem, dve_ysum[l, n])
                for n in range(KT):
                    dve.wait_ge(filled.sem, filled[("wo", l, n)])
                    at = place(("wo", l, n))
                    dve.wait_ge(s_xres[n % 2], 16 * (4 * l + n // 2 + 1))
                    stt3(hT[:, n, 0:TS], psum[:, at:at + TS], mod[:, 16 + n, 0:1], xres[n % 2][:, 0:TS],
                         ALU.mult, ALU.add)
                    ins = stt3(hT[:, n, TS:T], psum[:, at + TS:at + T], mod[:, 16 + n, 1:2], xres[n % 2][:, TS:T],
                               ALU.mult, ALU.add)
                    ins.then_inc(dve_e.sem, dve_e.mark(("wo", l, n)))
                    dve.wait_ge(dve_e.sem, dve_e[("wo", l, n)])
                    mul(acts[:, n, :], hT[:, n, :], hT[:, n, :]).then_inc(dve_xsq.sem, dve_xsq.mark(l + 1, n))
            dve.wait_ge(act_xrs.sem, act_xrs[DEPTH])
            for n in range(KT):
                stt3(acts[:, n, :], hT[:, n, :], v("final_g", n), w_rs, ALU.mult, ALU.mult).then_inc(dve_y.sem, dve_y.mark(n))
    return values


_FLOATS = {"xT": (P, KT, T), "units": (DEPTH, NU, P, UNIT), "small": (DEPTH, P, NSM), "vec": (DEPTH, P, NV),
           "con": (P, NC), "masks": (P, NM * 2 * P)}
_OUTS = {"yT": (P, KT, T), "new_ckv": (DEPTH, P, TP), "new_kpe": (DEPTH, 32, TP), "new_rw": (DEPTH, PAIRS, P, 2 * P),
         "new_gla": (DEPTH, P, 4 * P)}


def program(nc):
    a = {n: nc.dram_tensor(n, s, F32, kind="ExternalInput").ap() for n, s in _FLOATS.items()}
    for n, s in _OUTS.items():
        a[n] = nc.dram_tensor(n, s, F32, kind="ExternalOutput").ap()
    a["x_keep"] = nc.dram_tensor("x_keep", (P, KT, T), F32, kind="Internal").ap()
    return a


def lay_out(x):
    f = {n: np.asarray(w) for n, w in x.items()}
    tiles = lambda w: w.reshape(-1, P, w.shape[-1] // P, P).transpose(2, 1, 0, 3)
    cols = lambda w: w.reshape(-1, P).T
    out = {}
    tok = np.concatenate([f["x_sample"][0], f["x_prompt"][0]], 0)
    out["xT"] = tok.T.reshape(KT, P, T).transpose(1, 0, 2)
    units, small, vec = [], [], []
    off = {}
    at = 0
    for n, w in (("r", 512), ("k", 512), ("v", 512), ("wdad", 128), ("g", 512), ("gq", 256), ("gk", 256),
                 ("gv", 512), ("gad", 16), ("gg", 512), ("qd", 256), ("kvd", 128), ("kpe", 32), ("mg", 512),
                 ("ma", D), ("mb", D), ("mc", D)):
        off[n] = at
        at += w
    for l in range(DEPTH):
        w_in = f["w_in"][l].reshape(KT, P, -1)
        w_out = tiles(f["w_out"][l])
        w_mod = f["w_mod"][l].reshape(4, 2, P, 6, 512).transpose(0, 2, 3, 1, 4).reshape(4, P, 6, KT, P)
        o = {n: tiles(f[n][l]) for n in ("rw_out", "gla_out", "mla_out")}
        us = np.zeros((NU, P, KT, P), np.float32)
        for u, (n, i) in enumerate(UNITS):
            if n == "mod":
                us[u] = w_mod[i % 4, :, i // 4]
            elif n == "wo":
                us[u] = w_out[i]
            elif n == "oab":
                us[u, :, 0:4], us[u, :, 4:8] = o["rw_out"][i], o["gla_out"][i]
            elif n == "oc":
                us[u, :, 0:4] = o["mla_out"][i]
            elif n == "misc":
                us[u, :, :, 0:16] = w_in[:, :, off["gad"]:off["gad"] + 16].transpose(1, 0, 2)
                us[u, :, :, 64:96] = w_in[:, :, off["kpe"]:off["kpe"] + 32].transpose(1, 0, 2)
            else:
                us[u] = w_in[:, :, off[n] + P * i:off[n] + P * i + P].transpose(1, 0, 2)
        units.append(us.reshape(NU, P, UNIT))
        s = np.zeros((P, NSM), np.float32)
        s[0:64, SM["w2a2"]:SM["w2a2"] + 1024] = f["rw_w2"][l].transpose(1, 0, 2).reshape(64, 1024)
        s[64:128, SM["w2a2"]:SM["w2a2"] + 1024] = f["rw_a2"][l].transpose(1, 0, 2).reshape(64, 1024)
        s[0:16, SM["gla_a2"]:SM["gla_a2"] + 512] = f["gla_a2"][l].transpose(1, 0, 2).reshape(16, 512)
        s[:, SM["wq"]:SM["wq"] + 1536] = f["mla_wq_up"][l].reshape(2, P, 768).transpose(1, 0, 2).reshape(P, 1536)
        kv = f["mla_wkv_up"][l].reshape(P, HEADS, 2, 64)
        s[:, SM["wk"]:SM["wk"] + 512] = kv[:, :, 0].reshape(P, 512)
        s[:, SM["wv"]:SM["wv"] + 512] = kv[:, :, 1].reshape(P, 512)
        s[:, SM["ckv"]:SM["ckv"] + PAST] = f["cache_ckv"][0, l].T
        s[64:96, SM["kpe"]:SM["kpe"] + PAST] = f["cache_kpe"][0, l].T
        for d in range(2):
            for h in range(HEADS):
                c = SM["s_rw"] + P * (4 * d + h // 2) + 64 * (h % 2)
                s[64 * (h % 2):64 * (h % 2) + 64, c:c + 64] = f["state_rwkv"][0, l, d, h].T
            for h in range(4):
                c = SM["s_gla"] + P * (2 * d + h // 2)
                s[64 * (h % 2):64 * (h % 2) + 64, c:c + P] = f["state_gla"][0, l, d, h]
        small.append(s)
        cc = np.stack([cols(f["c"][0]), cols(f["c_ctx"])], -1).reshape(P, 16)
        vec.append(np.concatenate([cols(f["rw_w0"][l]), cols(f["rw_a0"][l]), cols(f["rw_k_k"][l]), cols(f["rw_k_a"][l]),
                                   cols(f["rw_r_k"][l]), cols(f["rw_ln_g"][l]), cols(f["rw_ln_b"][l]),
                                   cols(f["gla_ab"][l]), cols(f["gla_norm_g"][l]), cols(f["mla_qn_g"][l]),
                                   cols(f["mla_kvn_g"][l]), cols(f["norm_g"][l]), cols(f["b_mod"][l]), cc,
                                   cols(f["final_g"])], 1))
    out["units"], out["small"], out["vec"] = np.stack(units), np.stack(small), np.stack(vec)
    out["con"], out["masks"] = constant_table(), mask_table()
    return {n: np.ascontiguousarray(w) for n, w in out.items()}


def kernel(**inputs):
    import concourse.bacc as bacc
    from concourse.bass_utils import run_bass_kernel_spmd

    seen = {}
    for _ in range(2):
        nc = bacc.Bacc("TRN2", target_bir_lowering=False, num_devices=1)
        seen = build(nc, program(nc), seen)
    r = run_bass_kernel_spmd(nc, [lay_out(inputs)], core_ids=[0]).results[0]
    y = r["yT"].transpose(2, 1, 0).reshape(T, D)
    new_ckv = r["new_ckv"].transpose(0, 2, 1)[None]
    new_kpe = r["new_kpe"].transpose(0, 2, 1)[None]
    s = r["new_rw"].reshape(DEPTH, PAIRS, 2, 64, 2, 2, 64)
    rw = np.stack([s[:, :, h, :, :, h, :] for h in range(2)], 2)
    rw = rw.transpose(0, 4, 1, 2, 5, 3).reshape(DEPTH, 2, HEADS, 64, 64)[None]
    g = r["new_gla"].reshape(DEPTH, 2, 64, 2, 2, P).transpose(0, 4, 3, 1, 2, 5).reshape(DEPTH, 2, 4, 64, P)[None]
    return (np.ascontiguousarray(y[TS:])[None], np.ascontiguousarray(y[:TS])[None], np.ascontiguousarray(new_ckv),
            np.ascontiguousarray(new_kpe), np.ascontiguousarray(rw), np.ascontiguousarray(g))
```
